# Optimizing a Trainium2 kernel written in Bass

```python
import jax, jax.numpy as jnp
from jax import lax
import numpy as np

D_MODEL = 2048
BATCH = 1
SEQ = 128
DEPTH = 1
DEC_BATCH = 1
DEC_SEQ = 256
PAST_LEN = 128

GRID_W = 64
HEAD_DIM = 128
H_A = 6
KV_A = 2
H_B = 6
KV_B = 2
WINDOW = 128
H_C = 4
NOPE_DIM = 128
ROPE_DIM = 64
V_DIM = 128
KV_RANK = 256
MIX_WIDTH = H_A * HEAD_DIM + H_B * HEAD_DIM + H_C * V_DIM
N_GROUPS = 4
EXPERTS_PER_GROUP = 8
N_EXPERTS = N_GROUPS * EXPERTS_PER_GROUP
TOP_K = 2
D_EXPERT = 512
Q_BLOCK = 128
MOE_BLOCK = 128
RMS_EPS = 1e-6
ROPE_THETA = 10000.0
NEG_INF = -1e30
PROJ_SIZES = (H_A * HEAD_DIM, KV_A * HEAD_DIM, KV_A * HEAD_DIM,
              H_B * HEAD_DIM, KV_B * HEAD_DIM, KV_B * HEAD_DIM,
              H_C * (NOPE_DIM + ROPE_DIM), KV_RANK, ROPE_DIM)
PROJ_WIDTH = sum(PROJ_SIZES)
PROJ_SPLITS = tuple(sum(PROJ_SIZES[:i + 1]) for i in range(len(PROJ_SIZES) - 1))

kernel_name = "hybrid_diffusion_prefix_trunk_step"

def rms_norm(x, g):
    x32 = x.astype(jnp.float32)
    y = x32 * lax.rsqrt(jnp.mean(x32 * x32, axis=-1, keepdims=True) + RMS_EPS)
    return (y * g.astype(jnp.float32)).astype(x.dtype)

def modulate(h, shift, scale):
    return h * (1 + scale) + shift

def adaln(cond, w_mod, b_mod):
    m = jax.nn.silu(cond) @ w_mod + b_mod
    return jnp.split(m[:, None, :], 6, axis=-1)

def axial_rope_tables(n_tokens, rot_dim):
    rows = n_tokens // GRID_W
    row = jnp.repeat(jnp.arange(rows, dtype=jnp.float32), GRID_W)
    col = jnp.tile(jnp.arange(GRID_W, dtype=jnp.float32), rows)
    axis_dim = rot_dim // 2
    inv_freq = ROPE_THETA ** (-jnp.arange(0, axis_dim, 2, dtype=jnp.float32) / axis_dim)
    ang = jnp.concatenate([row[:, None] * inv_freq, col[:, None] * inv_freq], axis=-1)
    return jnp.cos(ang), jnp.sin(ang)

def apply_rope(x, cos, sin):
    x32 = x.astype(jnp.float32)
    x1, x2 = x32[..., 0::2], x32[..., 1::2]
    c, s = cos[None, :, None, :], sin[None, :, None, :]
    out = jnp.stack([x1 * c - x2 * s, x1 * s + x2 * c], axis=-1).reshape(x.shape)
    return out.astype(x.dtype)

def rope_tail(x, cos, sin):
    return jnp.concatenate([x[..., :NOPE_DIM], apply_rope(x[..., NOPE_DIM:], cos, sin)], axis=-1)

def blocked_attention(q, k, v, sink=None):
    B, S, H, Dk = q.shape
    KV = k.shape[2]
    G = H // KV
    Dv = v.shape[-1]
    nb = S // Q_BLOCK
    scale = Dk ** -0.5
    qb = jnp.moveaxis(q.reshape(B, nb, Q_BLOCK, KV, G, Dk), 1, 0)

    def one_block(qblk):
        s = jnp.einsum("bqkgd,btkd->bkgqt", qblk, k, preferred_element_type=jnp.float32) * scale
        if sink is not None:
            sk = jnp.broadcast_to(sink.astype(jnp.float32).reshape(KV, G)[None, :, :, None, None],
                                  s.shape[:-1] + (1,))
            s = jnp.concatenate([s, sk], axis=-1)
        p = jax.nn.softmax(s, axis=-1)
        if sink is not None:
            p = p[..., :-1]
        return jnp.einsum("bkgqt,btkd->bqkgd", p.astype(v.dtype), v)

    out = lax.map(one_block, qb)
    return jnp.moveaxis(out, 0, 1).reshape(B, S, H, Dv)

def banded_attention(q, k, v, k_ctx, v_ctx, sink):
    B, S, H, Dh = q.shape
    KV = k.shape[2]
    G = H // KV
    T = k_ctx.shape[1]
    nb = S // Q_BLOCK
    span = Q_BLOCK + 2 * WINDOW
    scale = Dh ** -0.5
    pad = ((0, 0), (WINDOW, WINDOW), (0, 0), (0, 0))
    kp, vp = jnp.pad(k, pad), jnp.pad(v, pad)
    idx = (jnp.arange(nb) * Q_BLOCK)[:, None] + jnp.arange(span)[None, :]
    kb, vb = kp[:, idx], vp[:, idx]
    kpos = idx - WINDOW
    qpos = (jnp.arange(nb) * Q_BLOCK)[:, None] + jnp.arange(Q_BLOCK)[None, :]
    valid = ((kpos[:, None, :] >= 0) & (kpos[:, None, :] < S)
             & (jnp.abs(qpos[:, :, None] - kpos[:, None, :]) <= WINDOW))
    qb = q.reshape(B, nb, Q_BLOCK, KV, G, Dh)
    s_loc = jnp.einsum("bnqkgd,bntkd->bnkgqt", qb, kb, preferred_element_type=jnp.float32) * scale
    s_loc = jnp.where(valid[None, :, None, None], s_loc, NEG_INF)
    s_ctx = jnp.einsum("bnqkgd,btkd->bnkgqt", qb, k_ctx, preferred_element_type=jnp.float32) * scale
    s_sink = jnp.broadcast_to(sink.astype(jnp.float32).reshape(KV, G)[None, None, :, :, None, None],
                              s_loc.shape[:-1] + (1,))
    p = jax.nn.softmax(jnp.concatenate([s_loc, s_ctx, s_sink], axis=-1), axis=-1)
    p_loc = p[..., :span].astype(v.dtype)
    p_ctx = p[..., span:span + T].astype(v.dtype)
    o = (jnp.einsum("bnkgqt,bntkd->bnqkgd", p_loc, vb)
         + jnp.einsum("bnkgqt,btkd->bnqkgd", p_ctx, v_ctx))
    return o.reshape(B, S, H, Dh)

def mla_keys_values(ckv_n, k_rope, w_ukv, kn_gain):
    B, T, _ = ckv_n.shape
    kv = (ckv_n @ w_ukv).reshape(B, T, H_C, NOPE_DIM + V_DIM)
    k_nope, v = kv[..., :NOPE_DIM], kv[..., NOPE_DIM:]
    k = jnp.concatenate([k_nope, jnp.broadcast_to(k_rope[:, :, None, :], (B, T, H_C, ROPE_DIM))], axis=-1)
    return rms_norm(k, kn_gain), v

def split_projection(h, w_in):
    B, S, _ = h.shape
    z = h @ w_in
    a_q, a_k, a_v, b_q, b_k, b_v, c_q, c_ckv, c_kr = jnp.split(z, PROJ_SPLITS, axis=-1)
    return (a_q.reshape(B, S, H_A, HEAD_DIM), a_k.reshape(B, S, KV_A, HEAD_DIM),
            a_v.reshape(B, S, KV_A, HEAD_DIM), b_q.reshape(B, S, H_B, HEAD_DIM),
            b_k.reshape(B, S, KV_B, HEAD_DIM), b_v.reshape(B, S, KV_B, HEAD_DIM),
            c_q.reshape(B, S, H_C, NOPE_DIM + ROPE_DIM), c_ckv, c_kr)

def merge_heads(o_a, o_b, o_c):
    B, S = o_a.shape[:2]
    return jnp.concatenate([o_a.reshape(B, S, -1), o_b.reshape(B, S, -1), o_c.reshape(B, S, -1)], axis=-1)

def context_mixer(h, lp):
    a_q, a_k, a_v, b_q, b_k, b_v, c_q, c_ckv, c_kr = split_projection(h, lp["w_in"])
    k_a = rms_norm(a_k, lp["a_kn"])
    k_b = rms_norm(b_k, lp["b_kn"])
    ckv_n = rms_norm(c_ckv, lp["c_kvn"])
    o_a = blocked_attention(rms_norm(a_q, lp["a_qn"]), k_a, a_v)
    o_b = blocked_attention(rms_norm(b_q, lp["b_qn"]), k_b, b_v, sink=lp["b_sink"])
    k_c, v_c = mla_keys_values(ckv_n, c_kr, lp["w_ukv"], lp["c_kn"])
    o_c = blocked_attention(rms_norm(c_q, lp["c_qn"]), k_c, v_c)
    out = merge_heads(o_a, o_b, o_c) @ lp["w_o"]
    return out, (k_a, a_v, k_b, b_v, ckv_n, c_kr)

def latent_mixer(h, ctx, lp, rope_hd, rope_r):
    ctx_a_k, ctx_a_v, ctx_b_k, ctx_b_v, ctx_ckv, ctx_kr = ctx
    a_q, a_k, a_v, b_q, b_k, b_v, c_q, c_ckv, c_kr = split_projection(h, lp["w_in"])
    q_a = apply_rope(rms_norm(a_q, lp["a_qn"]), *rope_hd)
    k_a = apply_rope(rms_norm(a_k, lp["a_kn"]), *rope_hd)
    o_a = blocked_attention(q_a, jnp.concatenate([ctx_a_k, k_a], axis=1),
                            jnp.concatenate([ctx_a_v, a_v], axis=1))
    q_b = apply_rope(rms_norm(b_q, lp["b_qn"]), *rope_hd)
    k_b = apply_rope(rms_norm(b_k, lp["b_kn"]), *rope_hd)
    o_b = banded_attention(q_b, k_b, b_v, ctx_b_k, ctx_b_v, lp["b_sink"])
    kc_ctx, vc_ctx = mla_keys_values(ctx_ckv, ctx_kr, lp["w_ukv"], lp["c_kn"])
    kc_lat, vc_lat = mla_keys_values(rms_norm(c_ckv, lp["c_kvn"]), c_kr, lp["w_ukv"], lp["c_kn"])
    kc_lat = rope_tail(kc_lat, *rope_r)
    q_c = rope_tail(rms_norm(c_q, lp["c_qn"]), *rope_r)
    o_c = blocked_attention(q_c, jnp.concatenate([kc_ctx, kc_lat], axis=1),
                            jnp.concatenate([vc_ctx, vc_lat], axis=1))
    return merge_heads(o_a, o_b, o_c) @ lp["w_o"]

def grouped_expert_mlp(hf, expert_id, e_w, w1, w3, w2):
    M, D = hf.shape
    n_assign = M * TOP_K
    flat_e = expert_id.reshape(-1)
    flat_tok = jnp.arange(n_assign, dtype=jnp.int32) // TOP_K
    flat_w = e_w.reshape(-1)
    order = jnp.argsort(flat_e)
    se, stok, sw = flat_e[order], flat_tok[order], flat_w[order]
    counts = jnp.bincount(flat_e, length=N_EXPERTS)
    pcounts = (counts + MOE_BLOCK - 1) // MOE_BLOCK * MOE_BLOCK
    pends = jnp.cumsum(pcounts)
    pstarts = pends - pcounts
    starts = jnp.cumsum(counts) - counts
    dest = pstarts[se] + jnp.arange(n_assign, dtype=jnp.int32) - starts[se]
    n_blocks = -(-(n_assign + N_EXPERTS * (MOE_BLOCK - 1)) // MOE_BLOCK)
    slot_tok = jnp.full((n_blocks * MOE_BLOCK,), M, jnp.int32).at[dest].set(stok)
    block_start = jnp.arange(n_blocks) * MOE_BLOCK
    block_expert = jnp.minimum(jnp.sum(pends[None, :] <= block_start[:, None], axis=1), N_EXPERTS - 1)
    h_pad = jnp.concatenate([hf, jnp.zeros((1, D), hf.dtype)], axis=0)
    xb = h_pad[slot_tok].reshape(n_blocks, MOE_BLOCK, D)

    def run_block(args):
        xblk, e = args
        return (jax.nn.silu(xblk @ w1[e]) * (xblk @ w3[e])) @ w2[e]

    yb = lax.map(run_block, (xb, block_expert)).reshape(n_blocks * MOE_BLOCK, D)
    return jax.ops.segment_sum(yb[dest] * sw[:, None].astype(yb.dtype), stok, num_segments=M)

def hier_moe(h, lp):
    B, S, D = h.shape
    M = B * S
    hf = h.reshape(M, D)
    g_logits = jnp.dot(hf, lp["w_rg"], preferred_element_type=jnp.float32) + lp["b_rg"].astype(jnp.float32)
    g_prob = jax.nn.softmax(g_logits, axis=-1)
    g_top_p, g_top = lax.top_k(g_prob, 1)
    e_logits = (jnp.dot(hf, lp["w_re"], preferred_element_type=jnp.float32)
                + lp["b_re"].astype(jnp.float32)).reshape(M, N_GROUPS, EXPERTS_PER_GROUP)
    e_in_group = jnp.take_along_axis(e_logits, g_top[:, :, None], axis=1)[:, 0]
    e_top_logit, e_top = lax.top_k(e_in_group, TOP_K)
    e_w = jax.nn.softmax(e_top_logit, axis=-1) * g_top_p
    expert_id = (g_top * EXPERTS_PER_GROUP + e_top).astype(jnp.int32)
    y = grouped_expert_mlp(hf, expert_id, e_w, lp["w1"], lp["w3"], lp["w2"])
    return y.reshape(B, S, D)

def setup_inputs(seed: int = 0) -> dict:
    key = jax.random.key(seed)
    ks = iter(jax.random.split(key, 40))
    f32 = jnp.float32

    def nrm(shape, scale=1.0):
        return jax.random.normal(next(ks), shape, f32) * scale

    def gain(shape):
        return 1.0 + 0.02 * nrm(shape)

    D = D_MODEL
    return {
        "x_prompt": nrm((BATCH, SEQ, D)),
        "x_sample": nrm((DEC_BATCH, DEC_SEQ, D)),
        "cache_a_k": nrm((DEC_BATCH, DEPTH, PAST_LEN, KV_A, HEAD_DIM)),
        "cache_a_v": nrm((DEC_BATCH, DEPTH, PAST_LEN, KV_A, HEAD_DIM)),
        "cache_b_k": nrm((DEC_BATCH, DEPTH, PAST_LEN, KV_B, HEAD_DIM)),
        "cache_b_v": nrm((DEC_BATCH, DEPTH, PAST_LEN, KV_B, HEAD_DIM)),
        "cache_c_kv": nrm((DEC_BATCH, DEPTH, PAST_LEN, KV_RANK)),
        "cache_c_krope": nrm((DEC_BATCH, DEPTH, PAST_LEN, ROPE_DIM)),
        "c": nrm((DEC_BATCH, D)),
        "c_ctx": nrm((D,)),
        "g_attn": gain((DEPTH, D)),
        "g_ffn": gain((DEPTH, D)),
        "w_mod": nrm((DEPTH, D, 6 * D), 0.5 * D ** -0.5),
        "b_mod": nrm((DEPTH, 6 * D), 0.01),
        "w_in": nrm((DEPTH, D, PROJ_WIDTH), D ** -0.5),
        "a_qn": gain((DEPTH, HEAD_DIM)),
        "a_kn": gain((DEPTH, HEAD_DIM)),
        "b_qn": gain((DEPTH, HEAD_DIM)),
        "b_kn": gain((DEPTH, HEAD_DIM)),
        "b_sink": nrm((DEPTH, H_B), 0.5),
        "c_kvn": gain((DEPTH, KV_RANK)),
        "w_ukv": nrm((DEPTH, KV_RANK, H_C * (NOPE_DIM + V_DIM)), KV_RANK ** -0.5),
        "c_qn": gain((DEPTH, NOPE_DIM + ROPE_DIM)),
        "c_kn": gain((DEPTH, NOPE_DIM + ROPE_DIM)),
        "w_o": nrm((DEPTH, MIX_WIDTH, D), MIX_WIDTH ** -0.5),
        "w_rg": nrm((DEPTH, D, N_GROUPS), D ** -0.5),
        "b_rg": nrm((DEPTH, N_GROUPS), 0.01),
        "w_re": nrm((DEPTH, D, N_EXPERTS), D ** -0.5),
        "b_re": nrm((DEPTH, N_EXPERTS), 0.01),
        "w1": nrm((DEPTH, N_EXPERTS, D, D_EXPERT), D ** -0.5),
        "w3": nrm((DEPTH, N_EXPERTS, D, D_EXPERT), D ** -0.5),
        "w2": nrm((DEPTH, N_EXPERTS, D_EXPERT, D), D_EXPERT ** -0.5),
    }

def reference(x_prompt, x_sample, cache_a_k, cache_a_v, cache_b_k, cache_b_v, cache_c_kv, cache_c_krope,
              c, c_ctx, g_attn, g_ffn, w_mod, b_mod, w_in, a_qn, a_kn, b_qn, b_kn, b_sink,
              c_kvn, w_ukv, c_qn, c_kn, w_o, w_rg, b_rg, w_re, b_re, w1, w3, w2):
    layers = [dict(g_attn=g_attn[l], g_ffn=g_ffn[l], w_mod=w_mod[l], b_mod=b_mod[l], w_in=w_in[l],
                   a_qn=a_qn[l], a_kn=a_kn[l], b_qn=b_qn[l], b_kn=b_kn[l], b_sink=b_sink[l],
                   c_kvn=c_kvn[l], w_ukv=w_ukv[l], c_qn=c_qn[l], c_kn=c_kn[l], w_o=w_o[l],
                   w_rg=w_rg[l], b_rg=b_rg[l], w_re=w_re[l], b_re=b_re[l],
                   w1=w1[l], w3=w3[l], w2=w2[l]) for l in range(DEPTH)]

    xp = x_prompt
    cond_ctx = c_ctx[None, :]
    st = [[], [], [], [], [], []]
    for l in range(DEPTH):
        lp = layers[l]
        sh1, sc1, g1, sh2, sc2, g2 = adaln(cond_ctx, lp["w_mod"], lp["b_mod"])
        mix, ctx_t = context_mixer(modulate(rms_norm(xp, lp["g_attn"]), sh1, sc1), lp)
        xp = xp + g1 * mix
        xp = xp + g2 * hier_moe(modulate(rms_norm(xp, lp["g_ffn"]), sh2, sc2), lp)
        for lst, t in zip(st, ctx_t):
            lst.append(t)
    state_a_k = jnp.stack(st[0], axis=1)
    state_a_v = jnp.stack(st[1], axis=1)
    state_b_k = jnp.stack(st[2], axis=1)
    state_b_v = jnp.stack(st[3], axis=1)
    state_c_kv = jnp.stack(st[4], axis=1)
    state_c_krope = jnp.stack(st[5], axis=1)

    xs = x_sample
    n_lat = xs.shape[1]
    rope_hd = axial_rope_tables(n_lat, HEAD_DIM)
    rope_r = axial_rope_tables(n_lat, ROPE_DIM)
    for l in range(DEPTH):
        lp = layers[l]
        sh1, sc1, g1, sh2, sc2, g2 = adaln(c, lp["w_mod"], lp["b_mod"])
        ctx = (cache_a_k[:, l], cache_a_v[:, l], cache_b_k[:, l], cache_b_v[:, l],
               cache_c_kv[:, l], cache_c_krope[:, l])
        mix = latent_mixer(modulate(rms_norm(xs, lp["g_attn"]), sh1, sc1), ctx, lp, rope_hd, rope_r)
        xs = xs + g1 * mix
        xs = xs + g2 * hier_moe(modulate(rms_norm(xs, lp["g_ffn"]), sh2, sc2), lp)

    return (xp, xs, state_a_k, state_a_v, state_b_k, state_b_v, state_c_kv, state_c_krope)


_drawn_inputs = setup_inputs


def setup_inputs(seed=0):
    import zlib

    import numpy as np

    out = dict(_drawn_inputs(seed))
    spreads = {}
    factors = {'cache_a_k': 7.321,
     'cache_a_v': 5.817,
     'cache_b_k': 5.639,
     'cache_b_v': 4.372,
     'cache_c_kv': 7.426,
     'cache_c_krope': 8.0,
     'g_attn': 2.902,
     'g_ffn': 4.565,
     'b_mod': 4.111,
     'a_qn': 8.0,
     'a_kn': 2.772,
     'b_qn': 8.0,
     'b_kn': 3.016,
     'b_sink': 8.0,
     'c_kvn': 2.873,
     'c_qn': 8.0,
     'c_kn': 8.0,
     'b_rg': 8.0,
     'b_re': 8.0}
    for name, (base, spread) in spreads.items():
        noise = np.random.default_rng([zlib.crc32(name.encode()), seed]).standard_normal(out[name].shape)
        drawn = base * np.exp(spread * noise) if base else spread * noise
        out[name] = __import__('jax').numpy.asarray(drawn.astype(out[name].dtype))
    for name, factor in factors.items():
        out[name] = (out[name] * factor).astype(out[name].dtype)
    return out
```

```python
from contextlib import ExitStack

import concourse.bass as bass
import numpy as np
from concourse import mybir

F32 = mybir.dt.float32
I32 = mybir.dt.int32
ACT = mybir.ActivationFunctionType
ALU = mybir.AluOpType
AX = mybir.AxisListType.X

P = 128
D = 2048
TILES = 3
T = TILES * P
KD = D // P
HD = 128
HEADS_A, HEADS_B, HEADS_C = 6, 6, 4
HEADS = HEADS_A + HEADS_B + HEADS_C
ROPE = 64
KV_RANK = 256
GRID_W = 64
EPS = 1e-6
THETA = 10000.0
NEG = -1e30
GROUPS, PER_GROUP = 4, 8
EXPERTS = GROUPS * PER_GROUP
TOP_K = 2
FF = 512
CAP = 64
MAX_Q = T // CAP
ITEMS = EXPERTS + (T * TOP_K - EXPERTS) // CAP + 1
ASSIGN = TOP_K * TILES
MISSING = 4096.0

SLOTS = 12
MOE_UNITS = 12
HALF = D // 2

Q_A, K_A, V_A = 0, 768, 1024
Q_B, K_B, V_B = 1280, 2048, 2304
Q_C, CKV, KR = 2560, 3328, 3584

CHUNKS = [("ckv", CKV, 320), ("cq0", Q_C, 384), ("cq1", Q_C + 384, 384),
          ("aq0", Q_A, 384), ("aq1", Q_A + 384, 384), ("bq0", Q_B, 384),
          ("akv", K_A, 512), ("bq1", Q_B + 384, 384), ("bkv", K_B, 512)]

SH1, SC1, G1, SH2, SC2, G2 = range(6)


def const_layout():
    at, out = 0, {}
    for name, n in (("ident", P), ("tri", P), ("ones", P), ("mask", 2 * P), ("cos", 2 * 64), ("sin", 2 * 64),
                    ("cosr", 2 * 32), ("sinr", 2 * 32), ("half", 1), ("items", ITEMS), ("slots", P),
                    ("rev32", EXPERTS), ("rev4", GROUPS), ("experts", EXPERTS), ("tok", ASSIGN),
                    ("dest", ASSIGN), ("pow", 4)):
        out[name] = (at, n)
        at += n
    return out, at


def constants():
    lay, n = const_layout()
    c = np.zeros((P, n), np.float32)

    def put(name, v):
        at, w = lay[name]
        c[:, at:at + w] = np.asarray(v, np.float32).reshape(-1, w)

    p = np.arange(P)
    put("ident", np.eye(P))
    put("tri", p[:, None] < p[None, :])
    put("ones", np.ones((P, P)))
    put("mask", np.concatenate([np.where(p[None, :] <= p[:, None], 0.0, NEG),
                                np.where(p[:, None] <= p[None, :], 0.0, NEG)], 1))
    tok = np.arange(2 * P)
    for dim, cn, sn in ((HD, "cos", "sin"), (ROPE, "cosr", "sinr")):
        axis = dim // 2
        inv = np.float32(THETA) ** (-np.arange(0, axis, 2, dtype=np.float32) / np.float32(axis))
        row, col = (tok // GRID_W).astype(np.float32), (tok % GRID_W).astype(np.float32)
        ang = np.concatenate([row[:, None] * inv, col[:, None] * inv], 1).astype(np.float32)
        for name, v in ((cn, np.cos(ang)), (sn, np.sin(ang))):
            put(name, v.reshape(2, P, axis).transpose(1, 0, 2).reshape(P, -1))
    put("half", (p // CAP)[:, None])
    put("items", np.arange(ITEMS)[None])
    put("slots", (p % CAP)[None])
    put("rev32", EXPERTS - np.arange(EXPERTS)[None])
    put("rev4", GROUPS - np.arange(GROUPS)[None])
    put("experts", np.arange(EXPERTS)[None])
    t = np.arange(TILES)[None] * P + p[:, None]
    put("tok", np.concatenate([t] * TOP_K, 1) - MISSING)
    put("dest", np.concatenate([k * T + t for k in range(TOP_K)], 1) - MISSING)
    put("pow", -0.5 * np.ones((P, 4)))
    return c


def plan():
    steps, jobs, atts = [], [], []
    units = []

    def mod(g, ks):
        for k in ks:
            units.append(("mod", g, k))
            steps.append(("mod", g, k))

    mod(SH1, range(KD))
    mod(SC1, range(KD))
    steps.append(("hmod",))
    later = [(g, k) for g in (G1, SH2, SC2) for k in range(KD)]
    pending = []

    def job(kind, what):
        jobs.append(what)
        steps.append((kind, len(jobs) - 1))
        if pending:
            steps.append(("turn", pending.pop()))
        pending.append(len(jobs) - 1)

    def kvc(tt, pair):
        job("kvc", ("kvc", tt, pair))

    def attend(group, heads, tiles=range(TILES)):
        new = [(group, h, t) for h in heads for t in tiles]
        first = len(atts)
        atts.extend(new)
        n = len(atts)
        for u in range(first, n + 1):
            if u < n:
                steps.append(("qk", u))
            if u > first:
                steps.append(("pt", u - 1))
                steps.append(("pv", u - 1))

    kvcs = [(tt, pair) for tt in range(4) for pair in range(2)]
    for name, _, _ in CHUNKS:
        units.extend([("in", name, i) for i in range(4)])
        for t in range(TILES):
            job("proj", (name, t))
            if name == "cq0" and t == 0:
                steps.append(("cache", "c"))
            if name == "cq0":
                for _ in range(min(3, len(kvcs))):
                    job("kvc", ("kvc", *kvcs.pop(0)))
            if name == "akv" and t == 0:
                steps.append(("cache", "a"))
            for g, k in later[:2]:
                mod(g, [k])
            del later[:2]
            if name == "aq0" and t:
                attend("C", [t - 1])
            if name == "aq1" and t < 2:
                attend("C", [t + 2])
            if name == "bq1":
                attend("A", [2 * t])
            if name == "bkv":
                attend("A", [2 * t + 1])
        if name == "ckv":
            units.append(("ukv",))
    steps.append(("cache", "b"))
    steps.append(("turn", pending.pop()))
    attend("B", range(HEADS_B))
    for cc in range(4):
        units.extend([("out", cc, i) for i in range(4)])
        for t in range(TILES):
            steps.append(("out", cc, t))
    mod(G2, range(KD))
    return steps, jobs, atts, units


IN_NAMES = ["x_prompt", "x_sample", "cache_a_k", "cache_a_v", "cache_b_k", "cache_b_v", "cache_c_kv",
            "cache_c_krope", "c", "c_ctx", "g_attn", "g_ffn", "w_mod", "b_mod", "w_in", "a_qn", "a_kn",
            "b_qn", "b_kn", "b_sink", "c_kvn", "w_ukv", "c_qn", "c_kn", "w_o", "w_rg", "b_rg", "w_re",
            "b_re", "w1", "w3", "w2"]
OUTS = [("y_prompt", (1, P, D)), ("y_sample", (1, 2 * P, D)),
        ("state_a_k", (1, 1, P, 2, HD)), ("state_a_v", (1, 1, P, 2, HD)),
        ("state_b_k", (1, 1, P, 2, HD)), ("state_b_v", (1, 1, P, 2, HD)),
        ("state_c_kv", (1, 1, P, KV_RANK)), ("state_c_krope", (1, 1, P, ROPE))]


def build(nc, ins, outs):
    steps, jobs, atts, units = plan()
    lay, n_const = const_layout()
    chunk_at = {name: (at, w) for name, at, w in CHUNKS}
    unit_no = {u: m for m, u in enumerate(units)}
    n_static = len(units)
    n_jobs, n_atts = len(jobs), len(atts)

    key_tile = [0, 2, 3]

    tp_no, n_tp = {}, KD
    last_turn, turn_before = n_tp, {}
    for s in steps:
        if s[0] in ("turn", "cache", "pt"):
            tp_no[s] = n_tp
            n_tp += 1
            if s[0] != "pt":
                last_turn = n_tp
        if s[0] == "qk":
            turn_before[s[1]] = last_turn
    groups_order = [SH1, SC1, G1, SH2, SC2, G2]

    def attention_of(u):
        g, h, t = atts[u]
        keys = slice(0, P) if t == 0 else slice(P, 4 * P)
        tiles = [0] if t == 0 else [1, 2, 3]
        return g, h, t, keys, tiles

    with ExitStack() as ctx:
        def sb(name, shape, dt=F32):
            return ctx.enter_context(nc.sbuf_tensor(name, shape, dt))

        def sem(name):
            return ctx.enter_context(nc.semaphore(name))

        ring = sb("ring", [P, SLOTS, D])
        r1 = sb("r1", [P, TILES * D])
        r2 = sb("r2", [P, TILES * D])
        r3 = sb("r3", [P, 6 * D])
        cst = sb("cst", [P, n_const])
        gains = sb("gains", [P, 1200])
        csil = sb("csil", [P, KD, 2])
        cvec = sb("cvec", [P, 2, KD])
        mod_row = sb("mod_row", [P, 512])
        gain_row = sb("gain_row", [P, 512])
        mod_t = sb("mod_t", [P, 2, 2, KD])
        small = sb("small", [P, 80])
        n_items = sb("n_items", [1, 1], I32)
        expert_of = sb("expert_of", [1, ITEMS], I32)
        gat_now = sb("gat_now", [P, 1], I32)
        sca_now = sb("sca_now", [P, 1], I32)

        def K(name):
            at, w = lay[name]
            return cst[:, at:at + w]

        ident, tri, ones = K("ident"), K("tri"), K("ones")
        h_t = r1[:].rearrange("p (k t) -> p k t", k=KD)
        x1 = r1[:].rearrange("p (t d) -> p t d", t=TILES)
        xn = r2[:].rearrange("p (t d) -> p t d", t=TILES)
        qo = r2[:].rearrange("p (t h q) -> p t h q", t=TILES, h=HEADS)
        h2 = xn

        at3 = [0]

        def r3_at(at, *shape):
            n = int(np.prod(shape))
            v = r3[:, at:at + n]
            names = "abcd"[:len(shape)]
            return v.rearrange(f"p ({' '.join(names)}) -> p {' '.join(names)}",
                               **dict(zip(names[:-1], shape[:-1])))

        def r3_next(*shape):
            v = r3_at(at3[0], *shape)
            at3[0] += int(np.prod(shape))
            assert at3[0] <= 6 * D
            return v

        k_c, v_c = r3_at(0, 4, 4 * P), r3_at(2048, 4, 4, HD)
        k_ab = {"A": r3_at(0, 2, 4 * P), "B": r3_at(2048, 2, 4 * P)}
        v_ab = {"A": r3_at(1024, 4, 2, HD), "B": r3_at(3072, 4, 2, HD)}
        at3[0] = 4096
        kr_c, qr_c = r3_next(2, 4 * P), r3_next(2, T)
        ckv_t = r3_next(2, 4 * P)
        zt = [r3_next(512), r3_next(512)]
        junk = r3_next(512)
        rope_tmp = r3_next(4, 192)
        prob = [r3_next(384), r3_next(384)]
        prob_t = [r3_next(3, P), r3_next(3, P)]
        kr, krg = r3_next(4, ROPE), r3_next(4, ROPE)
        junk_c = r3_next(ROPE)
        cached = {"c": r3_next(2 * P), "a": r3_next(2 * P), "b": r3_next(2 * P)}
        g1b, sh2b, a2b = (r3_at(i * 2 * D, 2, D) for i in range(3))
        h2_t = [r3_at(t * D, KD, P) for t in range(TILES)]
        g2b = r3_at(0, 2, D)
        xg, xg_t = r3_at(4096, HALF), r3_at(5120, 8, P)
        at3[0] = 6144
        lg = r3_next(TILES, GROUPS + EXPERTS)
        g_s, g_eq, g_oh, g_pen = (r3_next(TILES, GROUPS) for _ in range(4))
        sel, e_eq = r3_next(TILES, EXPERTS), r3_next(TILES, EXPERTS)
        oh = r3_next(ASSIGN, EXPERTS)
        oh_before = r3_next(ASSIGN + 1, EXPERTS)
        oh_tmp = r3_next(ASSIGN, EXPERTS)
        extra, extra_in, extra_ex, zero32 = (r3_next(EXPERTS) for _ in range(4))
        at_item = r3_next(ASSIGN, ITEMS)
        at_slot = r3_next(ASSIGN, P)
        vals = r3_next(ASSIGN, 3, ITEMS)
        tab_f = r3_next(2, ITEMS)
        tab_i = r3_next(2, ITEMS).bitcast(I32)
        w_tab = r3_next(ITEMS)
        over = r3_next(ITEMS - EXPERTS, EXPERTS)
        eid = r3_next(ITEMS)
        asg = r3_next(12, ASSIGN)
        tri3 = r3_next(12, TILES)
        sg, act = r3_next(256), r3_next(256)
        act_t = r3_next(2, P)
        y_sb = r3_next(2, 512)

        def y_in(k, t):
            return ring[:, k * TILES + t, :]

        off = [0]

        def gain(n):
            v = gains[:, off[0]:off[0] + n]
            off[0] += n
            return v

        gain_of = {n: gain(w) for n, w in (("a_qn", HD), ("a_kn", HD), ("b_qn", HD), ("b_kn", HD),
                                           ("c_kvn", KV_RANK), ("c_qn", 192), ("c_kn", 192))}
        sink = gain(HEADS_B)
        r_bias = gain(GROUPS + EXPERTS)
        junk2 = gains[:, 0:512]
        w_r = gains[:, 512:512 + KD * 36].rearrange("p (k n) -> p k n", k=KD)

        s_at = [0]

        def sm(n):
            v = small[:, s_at[0]:s_at[0] + n]
            s_at[0] += n
            return v

        ss, rstd = [sm(4), sm(4)], [sm(4), sm(4)]
        kr_ss = sm(4)
        mx, nmx, rsum, rinv, esink = ([sm(1), sm(1)] for _ in range(5))
        ssx, rx = sm(4), sm(4)
        ss2 = sm(12)
        ss2s, r2s = sm(4), sm(4)

        bank = [ctx.enter_context(nc.psum_tensor(f"bank{i}", [P, 512], F32)) for i in range(8)]
        acc, mod_ps, tp, sc_ps = bank[0:3], bank[3], bank[4:6], bank[6:8]
        n_acc = n_jobs + 4 * TILES
        lg_ps, rank_ps, tab_ps = (acc[(n_acc + i) % 3] for i in range(3))

        mod_d = nc.dram_tensor("mod_d", [6, 2, D], F32).ap()
        h2_d = nc.dram_tensor("h2_d", [T, D], F32).ap()
        y_d = nc.dram_tensor("y_d", [TOP_K * T, D], F32).ap()

        slot_full = [sem(f"slot_full{i}") for i in range(SLOTS)]
        slot_free = [sem(f"slot_free{i}") for i in range(SLOTS)]
        cond_in, x_in, const_in, gains_in = sem("cond_in"), sem("x_in"), sem("const_in"), sem("gains_in")
        cache_k_in, cache_v_in = sem("cache_k_in"), sem("cache_v_in")
        cleared, csil_ready = sem("cleared"), sem("csil_ready")
        row_in, mod_done, mod_read, row_scaled, row_out = (sem(n) for n in (
            "row_in", "mod_done", "mod_read", "row_scaled", "row_out"))
        modt_in = sem("modt_in")
        ssx_ready, rx_ready, xn_ready = sem("ssx_ready"), sem("rx_ready"), sem("xn_ready")
        tp_full, tp_read = sem("tp_full"), sem("tp_read")
        h_ready = sem("h_ready")
        acc_full = sem("acc_full")
        z_ready, rstd_ready, norm_ready, turned = (sem(n) for n in ("z_ready", "rstd_ready", "norm_ready", "turned"))
        krg_ready, krss_ready = sem("krg_ready"), sem("krss_ready")
        state_out = sem("state_out")
        s_full, nmax_ready, e_ready, p_ready, o_full, o_ready = (sem(n) for n in (
            "s_full", "nmax_ready", "e_ready", "p_ready", "o_full", "o_ready"))
        g1_in, sh2_in, a2_in, xres_in, wr_in = (sem(n) for n in ("g1_in", "sh2_in", "a2_in", "xres_in", "wr_in"))
        x1_ready, ss2_ready, ss2s_ready, r2_ready, h2_ready, h2_out = (sem(n) for n in (
            "x1_ready", "ss2_ready", "ss2s_ready", "r2_ready", "h2_ready", "h2_out"))
        ht_full, ht_read_a, ht_read_v = sem("ht_full"), sem("ht_read_a"), sem("ht_read_v")
        lg_full = sem("lg_full")
        ge_in, ge_out, re_in, re_out = sem("ge_in"), sem("ge_out"), sem("re_in"), sem("re_out")
        oh_ready, rank_full, vals_ready, tab_full, tab_ready = (sem(n) for n in (
            "oh_ready", "rank_full", "vals_ready", "tab_full", "tab_ready"))
        gidx, sidx, xg_in, xt_full, xt_read_a, xt_read_v = (sem(n) for n in (
            "gidx", "sidx", "xg_in", "xt_full", "xt_read_a", "xt_read_v"))
        xg_clear = sem("xg_clear")
        h1_full, h3_full, sg_ready, act_ready, at_full, at_read = (sem(n) for n in (
            "h1_full", "h3_full", "sg_ready", "act_ready", "at_full", "at_read"))
        y_full, y_read_a, y_read_v, y_out = sem("y_full"), sem("y_read_a"), sem("y_read_v"), sem("y_out")
        y_free, y_whole = sem("y_free"), sem("y_whole")
        yk_in = [sem(f"yk_in{t}") for t in range(TILES)]
        g2_in, final_ready, final_out = sem("g2_in"), sem("final_ready"), sem("final_out")
        v_step, p_step = sem("v_step"), sem("p_step")

        block = ctx.enter_context(nc.Block())

        def rows_in(n):
            return 32 * (n + 1 + (n >= SC1) + (n >= SC2))

        def unit_source(u, e=0):
            kind = u[0]
            if kind == "mod":
                _, g, k = u
                return (ins["w_mod"][0].rearrange("(p j) n -> p j n", j=KD)[:, k, g * D:(g + 1) * D], (D,))
            if kind == "in":
                _, name, i = u
                at, w = chunk_at[name]
                return (ins["w_in"][0].rearrange("(p j) n -> p j n", j=KD)[:, 4 * i:4 * i + 4, at:at + w], (4, w))
            if kind == "ukv":
                return ins["w_ukv"][0].rearrange("(j p) n -> p j n", j=2), (2, 1024)
            if kind == "out":
                _, cc, i = u
                return (ins["w_o"][0].rearrange("(j p) n -> p j n", p=P)[:, 4 * i:4 * i + 4, cc * 512:(cc + 1) * 512],
                        (4, 512))
            _, n = u
            if n < 8:
                w = ins["w1" if n < 4 else "w3"][0][bass.ds(e, 1)]
                half, j = (n % 4) // 2, 4 * (n % 2)
                return (w.rearrange("e (h p j) n -> h p (e j) n", h=2, j=8)[half][:, j:j + 4, :], (4, 512))
            w = ins["w2"][0][bass.ds(e, 1)]
            return w.rearrange("e (j p) n -> j p (e n)", p=P)[n - 8], (D,)

        def cut(slot, shape):
            v = ring[:, slot, 0:int(np.prod(shape))]
            return v if len(shape) == 1 else v.rearrange("p (a b) -> p a b", a=shape[0])

        frees, acc_uses, slot_uses = {}, 0, [0] * SLOTS
        for s in steps:
            if s[0] == "mod":
                m = unit_no[("mod", s[1], s[2])]
                if s[2] == KD - 1:
                    frees[m] = (mod_done, groups_order.index(s[1]) + 1)
                    continue
                done = [m]
            elif s[0] in ("proj", "kvc", "out"):
                acc_uses += 1
                last = False
                if s[0] == "proj" and jobs[s[1]][1] == TILES - 1:
                    own, last = [unit_no[("in", jobs[s[1]][0], i)] for i in range(4)], True
                elif s[0] == "out" and s[2] == TILES - 1:
                    own, last = [unit_no[("out", s[1], i)] for i in range(4)], True
                elif s[0] == "kvc" and jobs[s[1]][1:] == (3, 1):
                    own, last = [unit_no[("ukv",)]], True
                if not last:
                    continue
                frees[own[-1]] = (acc_full, acc_uses)
                done = own[:-1]
            else:
                continue
            for m in done:
                slot_uses[m % SLOTS] += 1
                frees[m] = (slot_free[m % SLOTS], slot_uses[m % SLOTS])
        assert sorted(frees) == list(range(n_static))
        moe_done = {3: h1_full, 7: h3_full, 11: y_full}

        @block.sync
        def _(sp):
            for m, u in enumerate(units):
                slot = m % SLOTS
                if m >= SLOTS:
                    sp.wait_ge(*frees[m - SLOTS])
                src, shape = unit_source(u)
                sp.dma_start(cut(slot, shape), src).then_inc(slot_full[slot], 16)

            for u in range(MOE_UNITS):
                slot = (n_static + u) % SLOTS
                sp.wait_ge(*frees[n_static + u - SLOTS])
                src, shape = unit_source(("moe", u), 0)
                sp.dma_start(cut(slot, shape), src).then_inc(slot_full[slot], 16)
            sp.wait_ge(tab_ready, 1)
            n = sp.value_load(n_items[0:1, 0:1], min_val=EXPERTS, max_val=ITEMS - 1)
            with sp.Fori(1, n) as i:
                e = sp.value_load(expert_of[0:1, bass.ds(i, 1)], min_val=0, max_val=EXPERTS - 1)
                for u in range(MOE_UNITS):
                    slot = (n_static + u) % SLOTS
                    if u in moe_done:
                        sp.wait_ge(moe_done[u], i + (1 if u == 11 else 0))
                    else:
                        sp.wait_ge(slot_free[slot], i + slot_uses[slot])
                    src, shape = unit_source(("moe", u), e)
                    sp.dma_start(cut(slot, shape), src).then_inc(slot_full[slot], 16)

            sp.wait_ge(y_out, n * 16)
            for t in range(TILES):
                for k in range(TOP_K):
                    sp.dma_start(y_in(k, t), y_d[k * T + t * P:k * T + (t + 1) * P, :]).then_inc(yk_in[t], 16)
            for t in range(TILES):
                sp.wait_ge(final_ready, t + 1)
                dst = outs["y_prompt"][0] if t == 0 else outs["y_sample"][0, (t - 1) * P:t * P, :]
                sp.dma_start(dst, x1[:, t, :]).then_inc(final_out, 16)
            sp.wait_ge(final_out, 16 * TILES)

        @block.tensor
        def _(pe):
            def arrived(m):
                pe.wait_ge(slot_full[m % SLOTS], (m // SLOTS + 1) * 16)

            pe.wait_ge(const_in, 16)
            pe.wait_ge(xn_ready, TILES)
            for k in range(KD):
                if k >= 2:
                    pe.wait_ge(tp_read, k - 1)
                for t in range(TILES):
                    mm = pe.transpose(tp[k % 2][:, t * P:(t + 1) * P], xn[:, t, k::KD], ident)
                mm.then_inc(tp_full, 1)

            pe.wait_ge(csil_ready, 1)

            def mod_step(g, k):
                m = unit_no[("mod", g, k)]
                arrived(m)
                n = groups_order.index(g)
                if k == 0 and n:
                    pe.wait_ge(mod_read, n)
                for q in range(4):
                    mm = pe.matmul(mod_ps[32 * q:32 * q + 2, :], csil[:, k, :], ring[:, m % SLOTS, q * 512:(q + 1) * 512],
                                   start=(k == 0), stop=(k == KD - 1))
                mm.then_inc(*((slot_free[m % SLOTS], 1) if k < KD - 1 else (mod_done, 1)))

            def acc_wait(a):
                if 3 <= a < n_jobs + 3:
                    pe.wait_ge(z_ready, a - 2)
                elif a >= n_jobs + 3:
                    pe.wait_ge(x1_ready, a - 2 - n_jobs)

            def tp_bank(s):
                n = tp_no[s]
                pe.wait_ge(tp_read, n - 1)
                return tp[n % 2]

            a = 0
            for s in steps:
                if s[0] == "mod" and s[1] != G2:
                    mod_step(s[1], s[2])
                elif s[0] == "proj":
                    name, t = jobs[s[1]]
                    w = chunk_at[name][1]
                    acc_wait(a)
                    for i in range(4):
                        m = unit_no[("in", name, i)]
                        arrived(m)
                        wu = cut(m % SLOTS, (4, w))
                        for j in range(4):
                            k = 4 * i + j
                            if a == 0:
                                pe.wait_ge(h_ready, k + 1)
                            mm = pe.matmul(acc[a % 3][:, 0:w], h_t[:, k, t * P:(t + 1) * P], wu[:, j, :],
                                           start=(k == 0), stop=(k == KD - 1))
                        if i == 3:
                            mm.then_inc(acc_full, 1)
                        elif t == TILES - 1:
                            mm.then_inc(slot_free[m % SLOTS], 1)
                    a += 1
                elif s[0] == "kvc":
                    _, tt, pair = jobs[s[1]]
                    acc_wait(a)
                    m = unit_no[("ukv",)]
                    arrived(m)
                    if tt == 1:
                        pe.wait_ge(tp_read, tp_no[("cache", "c")] + 1)
                    elif pair == 0:
                        t_job = jobs.index(("ckv", (0, None, 1, 2)[tt]))
                        pe.wait_ge(tp_read, tp_no[("turn", t_job)] + 1)
                    wu = cut(m % SLOTS, (2, 1024))
                    for j in range(2):
                        mm = pe.matmul(acc[a % 3][:, 0:512], ckv_t[:, j, tt * P:(tt + 1) * P],
                                       wu[:, j, pair * 512:(pair + 1) * 512], start=(j == 0), stop=(j == 1))
                    mm.then_inc(acc_full, 1)
                    a += 1
                elif s[0] == "turn":
                    n = s[1]
                    kind, z = jobs[n][0], zt[n % 2]
                    bankv = tp_bank(s)
                    pe.wait_ge(norm_ready, n + 1)
                    if kind in ("aq0", "aq1", "bq0", "bq1"):
                        cols = [0, P, 2 * P]
                    elif kind in ("cq0", "cq1"):
                        cols = [0, 192, 384]
                    elif kind == "kvc":
                        cols = [0, P, 2 * P]
                    else:
                        cols = [0, P]
                    for i, c in enumerate(cols):
                        mm = pe.transpose(bankv[:, i * P:(i + 1) * P], z[:, c:c + P], ident)
                    mm.then_inc(tp_full, 1)
                elif s[0] == "cache":
                    bankv = tp_bank(s)
                    pe.wait_ge(cache_k_in, 4 * 16)
                    for i in range(2):
                        mm = pe.transpose(bankv[:, i * P:(i + 1) * P], cached[s[1]][:, i * P:(i + 1) * P], ident)
                    mm.then_inc(tp_full, 1)
                elif s[0] == "qk":
                    u = s[1]
                    g, h, t, keys, _ = attention_of(u)
                    nk = keys.stop - keys.start
                    if u >= 2:
                        pe.wait_ge(o_ready, u - 1)
                    pe.wait_ge(tp_read, turn_before[u])
                    out = sc_ps[u % 2][:, 0:nk]
                    if g == "C":
                        pe.matmul(out, qo[:, t, 12 + h, :], k_c[:, h, keys], start=True, stop=False)
                        lo = 64 * (h % 2)
                        mm = pe.matmul(out, qr_c[lo:lo + 64, h // 2, t * P:(t + 1) * P],
                                       kr_c[lo:lo + 64, h // 2, keys], start=False, stop=True)
                    else:
                        hh = h + (HEADS_A if g == "B" else 0)
                        mm = pe.matmul(out, qo[:, t, hh, :], k_ab[g][:, h // 3, keys], start=True, stop=True)
                    mm.then_inc(s_full, 1)
                elif s[0] == "pt":
                    u = s[1]
                    _, _, _, _, tiles = attention_of(u)
                    bankv = tp_bank(s)
                    pe.wait_ge(p_ready, u + 1)
                    for i in range(len(tiles)):
                        mm = pe.transpose(bankv[:, i * P:(i + 1) * P], prob[u % 2][:, i * P:(i + 1) * P], ident)
                    mm.then_inc(tp_full, 1)
                elif s[0] == "pv":
                    u = s[1]
                    g, h, t, _, tiles = attention_of(u)
                    pe.wait_ge(tp_read, tp_no[("pt", u)] + 1)
                    if g != "C":
                        pe.wait_ge(cache_v_in, 2 * 16)
                    for i, tt in enumerate(tiles):
                        v = v_c[:, tt, h, :] if g == "C" else v_ab[g][:, tt, h // 3, :]
                        mm = pe.matmul(sc_ps[u % 2][:, 384:512], v, prob_t[u % 2][:, i, :],
                                       start=(i == 0), stop=(i == len(tiles) - 1))
                    mm.then_inc(o_full, 1)
                elif s[0] == "out":
                    _, cc, t = s
                    acc_wait(a)
                    if cc == 0 and t == 0:
                        pe.wait_ge(o_ready, n_atts)
                    for i in range(4):
                        m = unit_no[("out", cc, i)]
                        arrived(m)
                        wu = cut(m % SLOTS, (4, 512))
                        for j in range(4):
                            k = 4 * i + j
                            mm = pe.matmul(acc[a % 3][:, :], qo[:, t, k, :], wu[:, j, :],
                                           start=(k == 0), stop=(k == KD - 1))
                        if i == 3:
                            mm.then_inc(acc_full, 1)
                        elif t == TILES - 1:
                            mm.then_inc(slot_free[m % SLOTS], 1)
                    a += 1

            def turn_h2(t):
                pe.wait_ge(h2_ready, t + 1)
                for b in range(4):
                    if t:
                        pe.wait_ge(*((ht_read_a, 2 * t - 1 + b // 2) if b % 2 == 0 else (ht_read_v, 2 * t - 1 + b // 2)))
                    for i in range(4):
                        mm = pe.transpose(bank[4 + b][:, i * P:(i + 1) * P], h2[:, t, 4 * b + i::KD], ident)
                    mm.then_inc(ht_full, 1)

            def logits(t):
                pe.wait_ge(wr_in, 2 * 16)
                pe.wait_ge(ht_read_a, 2 * t + 2)
                pe.wait_ge(ht_read_v, 2 * t + 2)
                for k in range(KD):
                    mm = pe.matmul(lg_ps[:, t * 36:(t + 1) * 36], h2_t[t][:, k, :], w_r[:, k, :],
                                   start=(k == 0), stop=(k == KD - 1))
                if t == TILES - 1:
                    mm.then_inc(lg_full, 1)

            acc_wait(a)
            pe.wait_ge(tp_read, n_tp)
            for k in range(8):
                mod_step(G2, k)
            turn_h2(0)
            turn_h2(1)
            logits(0)
            logits(1)
            for k in range(8, 12):
                mod_step(G2, k)
            turn_h2(2)
            logits(2)
            for k in range(12, KD):
                mod_step(G2, k)

            pe.wait_ge(oh_ready, 1)
            pe.wait_ge(x1_ready, 12)
            pe.matmul(rank_ps[:, 0:192], tri, oh[:, :, :].rearrange("p a e -> p (a e)"), start=True, stop=False)
            pe.matmul(rank_ps[:, 0:192], ones, oh_before[:, 0:ASSIGN, :].rearrange("p a e -> p (a e)"),
                      start=False, stop=True)
            pe.matmul(rank_ps[:, 192:224], ones, oh_before[:, ASSIGN, :], start=True, stop=True).then_inc(rank_full, 1)

            pe.wait_ge(vals_ready, 1)
            for c in range(ASSIGN):
                mm = pe.matmul(tab_ps[:, 0:3 * ITEMS], at_slot[:, c, :], vals[:, c, :, :].rearrange("p v i -> p (v i)"),
                               start=(c == 0), stop=(c == ASSIGN - 1))
            mm.then_inc(tab_full, 1)

            def turn_x():
                for b in range(2):
                    for i in range(4):
                        mm = pe.transpose(tp[b][:, i * P:(i + 1) * P], xg[:, 4 * b + i::8], ident)
                mm.then_inc(xt_full, 1)

            pe.sem_inc(at_full, 1)
            pe.sem_inc(y_full, 1)
            pe.wait_ge(xg_in, 16)
            turn_x()
            pe.wait_ge(tab_ready, 1)
            n = pe.value_load(n_items[0:1, 0:1], min_val=EXPERTS, max_val=ITEMS - 1)
            with pe.Fori(0, n) as i:
                pe.wait_ge(xt_read_a, i + 1)
                pe.wait_ge(xt_read_v, i + 1)
                pe.wait_ge(act_ready, i + 1)
                for w, (ps, full) in enumerate(((acc[0], h1_full), (acc[1], h3_full))):
                    for uu in range(4):
                        u = 4 * w + uu
                        m = n_static + u
                        slot = m % SLOTS
                        pe.wait_ge(slot_full[slot], (i + m // SLOTS + 1) * 16)
                        half = uu // 2
                        for jj in range(4):
                            j = 4 * (uu % 2) + jj
                            for ct in range(2):
                                mm = pe.matmul(ps[64 * ct:64 * ct + 64, 0:256], xg_t[:, j, half * 64:half * 64 + 64],
                                               cut(slot, (4, 512))[:, jj, ct * 256:(ct + 1) * 256],
                                               start=(uu == 0 and jj == 0), stop=(uu == 3 and jj == 3))
                        mm.then_inc(full if uu == 3 else slot_free[slot], 1)
                pe.wait_ge(xg_in, i * 16 + 32)
                turn_x()
                pe.wait_ge(act_ready, i + 2)
                pe.wait_ge(at_read, i + 1)
                for q in range(2):
                    mm = pe.transpose(acc[2][:, q * P:(q + 1) * P], act[:, q * P:(q + 1) * P], ident)
                mm.then_inc(at_full, 1)
                pe.wait_ge(at_read, i + 2)
                pe.wait_ge(y_read_a, i + 1)
                pe.wait_ge(y_read_v, i + 1)
                for ft in range(4):
                    m = n_static + 8 + ft
                    slot = m % SLOTS
                    pe.wait_ge(slot_full[slot], (i + m // SLOTS + 1) * 16)
                    half, q = ft // 2, ft % 2
                    for c in range(2):
                        for ct in range(2):
                            mm = pe.matmul(sc_ps[c][64 * ct:64 * ct + 64, :], act_t[:, q, half * 64:half * 64 + 64],
                                           ring[:, slot, ct * HALF + c * 512:ct * HALF + (c + 1) * 512],
                                           start=(ft == 0), stop=(ft == 3))
                    mm.then_inc(y_full if ft == 3 else slot_free[slot], 1)

        @block.scalar
        def _(act_e):
            e = act_e
            e.dma_start(cvec[:, 0, :], ins["c_ctx"].rearrange("(p k) -> p k", k=KD)).then_inc(cond_in, 16)
            e.dma_start(cvec[:, 1, :], ins["c"][0].rearrange("(p k) -> p k", k=KD)).then_inc(cond_in, 16)
            e.dma_start(xn[:, 0, :], ins["x_prompt"][0]).then_inc(x_in, 16)
            e.dma_start(xn[:, 1:3, :], ins["x_sample"][0].rearrange("(t p) d -> p t d", p=P)).then_inc(x_in, 16)
            e.dma_start(cst[:], ins["consts"]).then_inc(const_in, 16)
            for name, v in gain_of.items():
                e.dma_start(v, ins[name][0].partition_broadcast(P)).then_inc(gains_in, 16)
            e.dma_start(sink, ins["b_sink"][0].partition_broadcast(P)).then_inc(gains_in, 16)
            e.dma_start(r_bias[:, 0:GROUPS], ins["b_rg"][0].partition_broadcast(P)).then_inc(gains_in, 16)
            e.dma_start(r_bias[:, GROUPS:], ins["b_re"][0].partition_broadcast(P)).then_inc(gains_in, 16)
            e.dma_start(cached["c"], ins["cache_c_kv"][0, 0]).then_inc(cache_k_in, 16)
            e.dma_start(kr[:, 1, :], ins["cache_c_krope"][0, 0]).then_inc(cache_k_in, 16)
            e.dma_start(cached["a"], ins["cache_a_k"][0, 0].rearrange("t h d -> t (h d)")).then_inc(cache_k_in, 16)
            e.dma_start(cached["b"], ins["cache_b_k"][0, 0].rearrange("t h d -> t (h d)")).then_inc(cache_k_in, 16)

            e.wait_ge(cond_in, 32)
            for c in range(2):
                e.activation(csil[:, :, c], cvec[:, c, :], ACT.Silu).then_inc(csil_ready, 1)

            e.wait_ge(x_in, 32)
            for t in range(TILES):
                e.activation(x1[:, t, :], xn[:, t, :], ACT.Square, accum_out=ssx[:, t:t + 1]).then_inc(ssx_ready, 1)
            e.wait_ge(ssx_ready, TILES)
            for k in range(KD):
                e.wait_ge(tp_full, k + 1)
                e.activation(h_t[:, k, :], tp[k % 2][:, 0:T], ACT.Copy).then_inc(tp_read, 1)

            states = 0
            a = 0
            for s in steps:
                if s[0] in ("proj", "kvc"):
                    n = s[1]
                    kind, z, ps = jobs[n][0], zt[n % 2], acc[a % 3]
                    e.wait_ge(acc_full, a + 1)
                    if n:
                        e.wait_ge(z_ready, n)
                    if n >= 2:
                        e.wait_ge(tp_full, tp_no[("turn", n - 2)] + 1)
                    if states:
                        e.wait_ge(state_out, 16 * states)
                    if kind in ("aq0", "aq1", "bq0", "bq1"):
                        heads, w = 3, HD
                    elif kind in ("cq0", "cq1"):
                        heads, w = 2, 192
                    elif kind == "kvc":
                        heads, w = 2, HD
                    elif kind == "ckv":
                        heads, w = 1, KV_RANK
                    else:
                        heads, w = 2, HD
                    step = 256 if kind == "kvc" else w
                    for i in range(heads):
                        e.activation(junk[:, i * w:(i + 1) * w] if i * w + w <= 512 else junk[:, 0:w],
                                     ps[:, i * step:i * step + w], ACT.Square,
                                     accum_out=ss[n % 2][:, i:i + 1])
                    if kind in ("akv", "bkv"):
                        g, t = kind[0].upper(), jobs[n][1]
                        if t == 0:
                            e.wait_ge(o_full, 12)
                        e.activation(v_ab[g][:, key_tile[t], :, :].rearrange("p h d -> p (h d)"), ps[:, 256:512], ACT.Copy)
                        last = e.activation(z[:, 0:256], ps[:, 0:256], ACT.Copy)
                    elif kind == "kvc":
                        _, tt, pair = jobs[n]
                        pv = ps[:, :].rearrange("p (h x) -> p h x", h=2)
                        e.activation(v_c[:, tt, 2 * pair:2 * pair + 2, :], pv[:, :, HD:], ACT.Copy)
                        last = e.activation(z[:, 0:256].rearrange("p (h x) -> p h x", h=2), pv[:, :, 0:HD], ACT.Copy)
                    elif kind == "ckv":
                        kt = key_tile[jobs[n][1]]
                        e.activation(junk[:, 256:320], ps[:, 256:320], ACT.Square, accum_out=kr_ss[:, kt:kt + 1])
                        e.activation(kr[:, kt, :], ps[:, 256:320], ACT.Copy)
                        last = e.activation(z[:, 0:256], ps[:, 0:256], ACT.Copy)
                    else:
                        last = e.activation(z[:, 0:384], ps[:, 0:384], ACT.Copy)
                    last.then_inc(z_ready, 1)
                    a += 1
                elif s[0] in ("turn", "cache"):
                    no = tp_no[s]
                    ps = tp[no % 2]
                    if s[0] == "turn":
                        n = s[1]
                        kind = jobs[n][0]
                        if kind in ("ckv", "akv", "bkv") and jobs[n][1] == 0:
                            e.wait_ge(norm_ready, n + 1)
                            if kind == "ckv":
                                e.dma_start(outs["state_c_kv"][0, 0], zt[n % 2][:, 0:256]).then_inc(state_out, 16)
                                e.dma_start(outs["state_c_krope"][0, 0], kr[:, 0, :]).then_inc(state_out, 16)
                            else:
                                g = kind[0]
                                e.dma_start(outs[f"state_{g}_k"][0, 0].rearrange("t h d -> t (h d)"),
                                            zt[n % 2][:, 0:256]).then_inc(state_out, 16)
                                e.dma_start(outs[f"state_{g}_v"][0, 0],
                                            v_ab[g.upper()][:, 0, :, :]).then_inc(state_out, 16)
                            states += 2
                    e.wait_ge(tp_full, no + 1)
                    if s[0] == "cache":
                        if s[1] == "c":
                            e.activation(junk_c, kr[:, 1, :], ACT.Square, accum_out=kr_ss[:, 1:2]).then_inc(krss_ready, 1)
                            dst = ckv_t[:, :, P:2 * P]
                        else:
                            dst = k_ab[s[1].upper()][:, :, P:2 * P]
                        last = e.activation(dst, ps[:, 0:256].rearrange("p (h x) -> p h x", h=2), ACT.Copy)
                    elif kind in ("aq0", "aq1", "bq0", "bq1"):
                        t = jobs[n][1]
                        h0 = {"aq0": 0, "aq1": 3, "bq0": 6, "bq1": 9}[kind]
                        last = e.activation(qo[:, t, h0:h0 + 3, :].rearrange("p h x -> p (h x)"), ps[:, 0:384], ACT.Copy)
                    elif kind in ("cq0", "cq1"):
                        t, pair = jobs[n][1], int(kind[2])
                        e.activation(qo[:, t, 12 + 2 * pair:14 + 2 * pair, :].rearrange("p h x -> p (h x)"),
                                     ps[:, 0:256], ACT.Copy)
                        last = e.activation(qr_c[:, pair, t * P:(t + 1) * P], ps[:, 256:384], ACT.Copy)
                    elif kind == "kvc":
                        _, tt, pair = jobs[n]
                        e.activation(k_c[:, 2 * pair:2 * pair + 2, tt * P:(tt + 1) * P],
                                     ps[:, 0:256].rearrange("p (h x) -> p h x", h=2), ACT.Copy)
                        last = e.activation(kr_c[:, pair, tt * P:(tt + 1) * P], ps[:, 256:384], ACT.Copy)
                    else:
                        kt = key_tile[jobs[n][1]]
                        dst = (ckv_t if kind == "ckv" else k_ab[kind[0].upper()])[:, :, kt * P:(kt + 1) * P]
                        last = e.activation(dst, ps[:, 0:256].rearrange("p (h x) -> p h x", h=2), ACT.Copy)
                    last.then_inc(tp_read, 1)
                elif s[0] == "qk":
                    u = s[1]
                    g, h, t, keys, _ = attention_of(u)
                    nk = keys.stop - keys.start
                    scale = (192 if g == "C" else HD) ** -0.5
                    e.wait_ge(nmax_ready, u + 1)
                    if u >= 2:
                        e.wait_ge(tp_full, tp_no[("pt", u - 2)] + 1)
                    if g == "B":
                        e.activation(esink[u % 2], sink[:, h:h + 1], ACT.Exp, bias=nmx[u % 2])
                    e.activation(prob[u % 2][:, 0:nk], sc_ps[u % 2][:, 0:nk], ACT.Exp, bias=nmx[u % 2], scale=scale,
                                 accum_out=rsum[u % 2]).then_inc(e_ready, 1)
                elif s[0] == "pt":
                    u = s[1]
                    _, _, _, _, tiles = attention_of(u)
                    no = tp_no[s]
                    e.wait_ge(tp_full, no + 1)
                    if u >= 2:
                        e.wait_ge(o_full, u - 1)
                    e.activation(prob_t[u % 2][:, 0:len(tiles), :].rearrange("p a b -> p (a b)"),
                                 tp[no % 2][:, 0:len(tiles) * P], ACT.Copy).then_inc(tp_read, 1)
                elif s[0] == "out":
                    _, cc, t = s
                    n = cc * TILES + t
                    e.wait_ge(x1_ready, n + 1)
                    if n:
                        e.wait_ge(ss2_ready, n)
                    e.activation(junk2, x1[:, t, cc * 512:(cc + 1) * 512], ACT.Square,
                                 accum_out=ss2[:, 4 * t + cc:4 * t + cc + 1]).then_inc(ss2_ready, 1)

            for t in range(TILES):
                for b in (0, 2):
                    e.wait_ge(ht_full, 4 * t + b + 1)
                    e.activation(h2_t[t][:, 4 * b:4 * b + 4, :].rearrange("p a b -> p (a b)"), bank[4 + b][:, :],
                                 ACT.Copy).then_inc(ht_read_a, 1)
            e.wait_ge(ge_in, 1)
            e.activation(g_s, g_s, ACT.Exp).then_inc(ge_out, 1)
            e.wait_ge(re_in, 1)
            e.activation(tri3[:, 5, :], tri3[:, 4, :], ACT.Exp).then_inc(re_out, 1)

            def x_out(i):
                e.wait_ge(xt_full, i + 1)
                e.activation(xg_t[:, 0:4, :].rearrange("p a b -> p (a b)"), tp[0][:, :], ACT.Copy).then_inc(xt_read_a, 1)

            e.sem_inc(y_read_a, 1)
            x_out(0)
            e.wait_ge(tab_ready, 1)
            n = e.value_load(n_items[0:1, 0:1], min_val=EXPERTS, max_val=ITEMS - 1)
            with e.Fori(0, n) as i:
                e.wait_ge(h1_full, i + 1)
                e.wait_ge(act_ready, i + 1)
                e.activation(sg, acc[0][:, 0:256], ACT.Silu).then_inc(sg_ready, 1)
                e.wait_ge(h3_full, i + 1)
                x_out(i + 1)
                e.wait_ge(y_full, i + 2)
                e.wait_ge(y_free, i + 1)
                e.activation(y_sb[:, 0, :], sc_ps[0][:, :], ACT.Copy, scale=w_tab[:, bass.ds(i, 1)]).then_inc(y_read_a, 1)

        @block.vector
        def _(v):
            own = [0]

            def after(ins):
                own[0] += 1
                ins.then_inc(v_step, 1)
                v.wait_ge(v_step, own[0])

            for t in range(TILES):
                v.wait_ge(rx_ready, t + 1)
                v.tensor_scalar(xn[:, t, :], xn[:, t, :], rx[:, t:t + 1], None, ALU.mult).then_inc(xn_ready, 1)

            def bc(x, *shape):
                return x.to_broadcast([P, *shape])

            def rope(z, heads, pairs, cos, sin, out_sem=None):
                zp = z.rearrange("p h (c two) -> p h c two", two=2)
                e0, e1 = zp[:, :, :, 0], zp[:, :, :, 1]
                cb = cos.unsqueeze(1).to_broadcast([P, heads, pairs])
                sb_ = sin.unsqueeze(1).to_broadcast([P, heads, pairs])
                tmp = [rope_tmp[:, i, 0:heads * pairs].rearrange("p (h c) -> p h c", h=heads) for i in range(4)]
                v.tensor_tensor(tmp[0], e0, cb, ALU.mult)
                v.tensor_tensor(tmp[1], e1, sb_, ALU.mult)
                v.tensor_tensor(tmp[2], e0, sb_, ALU.mult)
                after(v.tensor_tensor(tmp[3], e1, cb, ALU.mult))
                v.tensor_tensor(e0, tmp[0], tmp[1], ALU.subtract)
                return v.tensor_tensor(e1, tmp[2], tmp[3], ALU.add)

            def tables(t, names):
                c, s_ = K(names[0]), K(names[1])
                w = c.shape[-1] // 2
                return c[:, (t - 1) * w:t * w], s_[:, (t - 1) * w:t * w]

            first_gain = [True]

            def key_rope(kt, tile):
                last = v.tensor_tensor(krg[:, kt, :], kr[:, kt, :], gain_of["c_kn"][:, HD:192], ALU.mult)
                if tile:
                    after(last)
                    last = rope(krg[:, kt:kt + 1, :], 1, 32, *tables(tile, ("cosr", "sinr")))
                v.tensor_scalar(kr_ss[:, kt:kt + 1], kr_ss[:, kt:kt + 1], 192 * EPS, None, ALU.add).then_inc(krg_ready, 1)

            n_out = 0
            for s in steps:
                if s[0] == "mod" and s[2] == KD - 1 and s[1] != G2:
                    g = s[1]
                    n = groups_order.index(g)
                    v.wait_ge(mod_done, n + 1)
                    v.wait_ge(row_in, rows_in(n))
                    for q in range(4):
                        r = slice(32 * q, 32 * q + 2)
                        last = v.tensor_tensor(mod_row[r, :], mod_ps[r, :], mod_row[r, :], ALU.add)
                    last.then_inc(mod_read, 1)
                    if g in (SC1, SC2):
                        v.wait_ge(mod_read, n + 1)
                        for q in range(4):
                            r = slice(32 * q, 32 * q + 2)
                            last = v.scalar_tensor_tensor(out=mod_row[r, :], in0=mod_row[r, :], scalar=1.0,
                                                          in1=gain_row[r, :], op0=ALU.add, op1=ALU.mult)
                        last.then_inc(row_scaled, 1)
                elif s[0] == "hmod":
                    v.wait_ge(modt_in, 4 * 16)
                    v.wait_ge(tp_read, KD)
                    for k in range(KD):
                        v.tensor_scalar(h_t[:, k, 0:P], h_t[:, k, 0:P], mod_t[:, 1, 0, k:k + 1], mod_t[:, 0, 0, k:k + 1],
                                        ALU.mult, ALU.add)
                        v.tensor_scalar(h_t[:, k, P:T], h_t[:, k, P:T], mod_t[:, 1, 1, k:k + 1], mod_t[:, 0, 1, k:k + 1],
                                        ALU.mult, ALU.add).then_inc(h_ready, 1)
                elif s[0] in ("proj", "kvc"):
                    n = s[1]
                    kind, z, r = jobs[n][0], zt[n % 2], rstd[n % 2]
                    if n == 0:
                        v.wait_ge(gains_in, 10 * 16)
                    v.wait_ge(z_ready, n + 1)
                    v.wait_ge(rstd_ready, n + 1)

                    def scale_by(out, in_, i, gn):
                        return v.scalar_tensor_tensor(out=out, in0=in_, scalar=r[:, i:i + 1], in1=gn,
                                                      op0=ALU.mult, op1=ALU.mult)

                    if kind in ("aq0", "aq1", "bq0", "bq1", "akv", "bkv"):
                        heads = 3 if kind[1] == "q" else 2
                        gn = gain_of[kind[0] + ("_qn" if kind[1] == "q" else "_kn")]
                        for i in range(heads):
                            last = scale_by(z[:, i * HD:(i + 1) * HD], z[:, i * HD:(i + 1) * HD], i, gn)
                        if jobs[n][1]:
                            after(last)
                            last = rope(z[:, 0:heads * HD].rearrange("p (h x) -> p h x", h=heads), heads, 64,
                                        *tables(jobs[n][1], ("cos", "sin")))
                    elif kind in ("cq0", "cq1"):
                        for i in range(2):
                            scale_by(z[:, 384 + 64 * i:448 + 64 * i], z[:, i * 192 + HD:(i + 1) * 192], i,
                                     gain_of["c_qn"][:, HD:192])
                            last = scale_by(z[:, i * 192:i * 192 + HD], z[:, i * 192:i * 192 + HD], i,
                                            gain_of["c_qn"][:, 0:HD])
                        if jobs[n][1]:
                            after(last)
                            last = rope(z[:, 384:512].rearrange("p (h x) -> p h x", h=2), 2, 32,
                                        *tables(jobs[n][1], ("cosr", "sinr")))
                    elif kind == "ckv":
                        key_rope(key_tile[jobs[n][1]], jobs[n][1])
                        last = scale_by(z[:, 0:256], z[:, 0:256], 0, gain_of["c_kvn"])
                    else:
                        tt = jobs[n][1]
                        if n and jobs[n][2] == 0:
                            v.wait_ge(krg_ready, (1, 4, 2, 3)[tt])
                        for i in range(2):
                            scale_by(z[:, i * HD:(i + 1) * HD], z[:, i * HD:(i + 1) * HD], i, gain_of["c_kn"][:, 0:HD])
                            last = v.tensor_scalar(z[:, 256 + 64 * i:320 + 64 * i], krg[:, tt, :], r[:, i:i + 1], None, ALU.mult)
                    last.then_inc(norm_ready, 1)
                elif s == ("cache", "c"):
                    v.wait_ge(krss_ready, 1)
                    key_rope(1, 0)
                elif s[0] == "qk":
                    u = s[1]
                    g, h, t, keys, _ = attention_of(u)
                    nk = keys.stop - keys.start
                    b = u % 2
                    ps = sc_ps[b]
                    scale = (192 if g == "C" else HD) ** -0.5
                    v.wait_ge(s_full, u + 1)
                    if g == "B" and t:
                        lo = 2 * P if t == 1 else P
                        after(v.tensor_tensor(ps[:, lo:lo + P], ps[:, lo:lo + P], K("mask")[:, (t - 1) * P:t * P], ALU.add))
                    after(v.tensor_reduce(mx[b], ps[:, 0:nk], AX, ALU.max))
                    if g == "B":
                        after(v.tensor_scalar(mx[b], mx[b], scale, sink[:, h:h + 1], ALU.mult, ALU.max))
                        v.tensor_scalar(nmx[b], mx[b], -1.0, None, ALU.mult).then_inc(nmax_ready, 1)
                    else:
                        v.tensor_scalar(nmx[b], mx[b], -scale, None, ALU.mult).then_inc(nmax_ready, 1)
                    v.wait_ge(e_ready, u + 1)
                    if g == "B":
                        after(v.tensor_tensor(rsum[b], rsum[b], esink[b], ALU.add))
                    after(v.reciprocal(rinv[b], rsum[b]))
                    v.tensor_scalar(prob[b][:, 0:nk], prob[b][:, 0:nk], rinv[b], None, ALU.mult).then_inc(p_ready, 1)
                elif s[0] == "pv":
                    u = s[1]
                    g, h, t, _, _ = attention_of(u)
                    hh = h + {"A": 0, "B": HEADS_A, "C": HEADS_A + HEADS_B}[g]
                    v.wait_ge(o_full, u + 1)
                    v.tensor_copy(qo[:, t, hh, :], sc_ps[u % 2][:, 384:512]).then_inc(o_ready, 1)
                elif s[0] == "out":
                    _, cc, t = s
                    cond = min(t, 1)
                    ps = acc[(n_jobs + n_out) % 3]
                    if n_out == 0:
                        v.wait_ge(g1_in, 2 * 16)
                        v.wait_ge(xres_in, 2 * 16)
                    v.wait_ge(acc_full, n_jobs + n_out + 1)
                    after(v.tensor_tensor(ps[:, :], ps[:, :], g1b[:, cond, cc * 512:(cc + 1) * 512], ALU.mult))
                    xs = x1[:, t, cc * 512:(cc + 1) * 512]
                    v.tensor_tensor(xs, ps[:, :], xs, ALU.add).then_inc(x1_ready, 1)
                    n_out += 1
                    if cc == 3:
                        v.wait_ge(ss2_ready, n_out)
                        v.tensor_reduce(ss2s[:, t:t + 1], ss2[:, 4 * t:4 * t + 4], AX, ALU.add).then_inc(ss2s_ready, 1)
                        v.wait_ge(r2_ready, t + 1)
                        if t == 0:
                            v.wait_ge(a2_in, 2 * 16)
                            v.wait_ge(sh2_in, 2 * 16)
                        after(v.scalar_tensor_tensor(out=h2[:, t, :], in0=x1[:, t, :], scalar=r2s[:, t:t + 1],
                                                     in1=a2b[:, cond, :], op0=ALU.mult, op1=ALU.mult))
                        v.tensor_tensor(h2[:, t, :], h2[:, t, :], sh2b[:, cond, :], ALU.add).then_inc(h2_ready, 1)

            for t in range(TILES):
                for b in (1, 3):
                    v.wait_ge(ht_full, 4 * t + b + 1)
                    v.tensor_copy(h2_t[t][:, 4 * b:4 * b + 4, :].rearrange("p a b -> p (a b)"),
                                  bank[4 + b][:, :]).then_inc(ht_read_v, 1)
            v.wait_ge(lg_full, 1)
            after(v.tensor_tensor(lg, lg_ps[:, 0:108].rearrange("p (t n) -> p t n", t=TILES),
                                  r_bias.unsqueeze(1).to_broadcast([P, TILES, 36]), ALU.add))
            gl, el = lg[:, :, 0:GROUPS], lg[:, :, GROUPS:]
            gmax, gsum, gp, m0, m1, d_, den, rden, vm = (tri3[:, i, :] for i in (0, 1, 2, 3, 6, 4, 7, 8, 9))
            r_ = tri3[:, 5, :]

            def b3(x, n):
                return x.unsqueeze(2).to_broadcast([P, TILES, n])

            after(v.tensor_reduce(gmax, gl, AX, ALU.max))
            v.tensor_tensor(g_s, gl, b3(gmax, GROUPS), ALU.subtract).then_inc(ge_in, 1)
            after(v.tensor_tensor(g_eq, gl, b3(gmax, GROUPS), ALU.is_equal))
            after(v.tensor_tensor(g_eq, g_eq, K("rev4").unsqueeze(1).to_broadcast([P, TILES, GROUPS]), ALU.mult))
            after(v.tensor_reduce(vm, g_eq, AX, ALU.max))
            after(v.tensor_tensor(g_oh, g_eq, b3(vm, GROUPS), ALU.is_equal))
            after(v.tensor_scalar(g_pen, g_oh, -1.0, -NEG, ALU.add, ALU.mult))
            for t in range(TILES):
                after(v.tensor_tensor(sel[:, t, :].rearrange("p (g e) -> p g e", g=GROUPS),
                                      el[:, t, :].rearrange("p (g e) -> p g e", g=GROUPS),
                                      g_oh[:, t, :].unsqueeze(2).to_broadcast([P, GROUPS, PER_GROUP]), ALU.mult))
                after(v.tensor_tensor(sel[:, t, :].rearrange("p (g e) -> p g e", g=GROUPS),
                                      sel[:, t, :].rearrange("p (g e) -> p g e", g=GROUPS),
                                      g_pen[:, t, :].unsqueeze(2).to_broadcast([P, GROUPS, PER_GROUP]), ALU.add))
            for k in range(TOP_K):
                m_ = (m0, m1)[k]
                o_ = oh[:, k * TILES:(k + 1) * TILES, :]
                after(v.tensor_reduce(m_, sel, AX, ALU.max))
                after(v.tensor_tensor(e_eq, sel, b3(m_, EXPERTS), ALU.is_equal))
                after(v.tensor_tensor(e_eq, e_eq, K("rev32").unsqueeze(1).to_broadcast([P, TILES, EXPERTS]), ALU.mult))
                after(v.tensor_reduce(vm, e_eq, AX, ALU.max))
                after(v.tensor_tensor(o_, e_eq, b3(vm, EXPERTS), ALU.is_equal))
                if k == 0:
                    after(v.scalar_tensor_tensor(out=sel, in0=o_, scalar=2 * NEG, in1=sel, op0=ALU.mult, op1=ALU.add))
            after(v.memset(oh_before[:, 0, :], 0.0))
            for c in range(ASSIGN):
                last = v.tensor_tensor(oh_before[:, c + 1, :], oh_before[:, c, :], oh[:, c, :], ALU.add)
                if c < ASSIGN - 1:
                    after(last)
            last.then_inc(oh_ready, 1)
            v.memset(xg, 0.0).then_inc(xg_clear, 1)
            weight = asg[:, 0, :]
            v.tensor_tensor(d_, m1, m0, ALU.subtract).then_inc(re_in, 1)
            v.wait_ge(ge_out, 1)
            after(v.tensor_reduce(gsum, g_s, AX, ALU.add))
            after(v.reciprocal(gp, gsum))
            v.wait_ge(re_out, 1)
            after(v.tensor_scalar(den, r_, 1.0, None, ALU.add))
            after(v.reciprocal(rden, den))
            after(v.tensor_tensor(weight[:, 0:TILES], gp, rden, ALU.mult))
            after(v.tensor_tensor(weight[:, TILES:ASSIGN], weight[:, 0:TILES], r_, ALU.mult))

            rank, exp_a, ovb, q_, slot_a, item_a, tmp6 = (asg[:, i, :] for i in range(1, 8))
            v.wait_ge(rank_full, 1)
            cnt = rank_ps[:, 192:224]
            after(v.tensor_tensor(oh_tmp, oh, rank_ps[:, 0:192].rearrange("p (a e) -> p a e", a=ASSIGN), ALU.mult))
            after(v.tensor_reduce(rank, oh_tmp, AX, ALU.add))
            after(v.tensor_scalar(extra, cnt, float(CAP), None, ALU.is_gt))
            for j in range(2, MAX_Q):
                after(v.scalar_tensor_tensor(out=extra, in0=cnt, scalar=float(CAP * j), in1=extra,
                                             op0=ALU.is_gt, op1=ALU.add))
            after(v.memset(zero32, 0.0))
            after(v.tensor_tensor_scan(extra_in, zero32, extra, 0.0, ALU.add, ALU.add))
            after(v.tensor_tensor(extra_ex, extra_in, extra, ALU.subtract))
            after(v.tensor_tensor(oh_tmp, oh, K("experts").unsqueeze(1).to_broadcast([P, ASSIGN, EXPERTS]), ALU.mult))
            after(v.tensor_reduce(exp_a, oh_tmp, AX, ALU.add))
            after(v.tensor_tensor(oh_tmp, oh, extra_ex.unsqueeze(1).to_broadcast([P, ASSIGN, EXPERTS]), ALU.mult))
            after(v.tensor_reduce(ovb, oh_tmp, AX, ALU.add))
            after(v.tensor_scalar(q_, rank, float(CAP), None, ALU.is_ge))
            for j in range(2, MAX_Q):
                after(v.scalar_tensor_tensor(out=q_, in0=rank, scalar=float(CAP * j), in1=q_, op0=ALU.is_ge, op1=ALU.add))
            after(v.scalar_tensor_tensor(out=slot_a, in0=q_, scalar=-float(CAP), in1=rank, op0=ALU.mult, op1=ALU.add))
            after(v.tensor_tensor(tmp6, ovb, q_, ALU.add))
            after(v.scalar_tensor_tensor(out=tmp6, in0=tmp6, scalar=float(EXPERTS - 1), in1=exp_a,
                                         op0=ALU.add, op1=ALU.subtract))
            after(v.scalar_tensor_tensor(out=tmp6, in0=q_, scalar=1.0, in1=tmp6, op0=ALU.is_ge, op1=ALU.mult))
            after(v.tensor_tensor(item_a, exp_a, tmp6, ALU.add))

            def b6(x, n):
                return x.unsqueeze(2).to_broadcast([P, ASSIGN, n])

            v.tensor_tensor(at_slot, K("slots").unsqueeze(1).to_broadcast([P, ASSIGN, P]), b6(slot_a, P), ALU.is_equal)
            after(v.tensor_tensor(at_item, K("items").unsqueeze(1).to_broadcast([P, ASSIGN, ITEMS]),
                                  b6(item_a, ITEMS), ALU.is_equal))
            for i, x in enumerate((K("tok"), K("dest"), weight)):
                last = v.tensor_tensor(vals[:, :, i, :], at_item, b6(x, ITEMS), ALU.mult)
            last.then_inc(vals_ready, 1)
            n_over = ITEMS - EXPERTS
            v.tensor_copy(eid[0:1, 0:EXPERTS], K("experts")[0:1, :])
            after(v.tensor_scalar(eid[0:1, EXPERTS:], K("items")[0:1, 0:n_over], 0.0, None, ALU.add))
            after(v.tensor_tensor(over[0:1], extra_in[0:1].unsqueeze(1).to_broadcast([1, n_over, EXPERTS]),
                                  eid[0:1, EXPERTS:].unsqueeze(2).to_broadcast([1, n_over, EXPERTS]), ALU.is_le))
            after(v.tensor_reduce(eid[0:1, EXPERTS:], over[0:1], AX, ALU.add))
            after(v.tensor_scalar(eid[0:1, EXPERTS:], eid[0:1, EXPERTS:], float(EXPERTS - 1), None, ALU.min))
            v.tensor_copy(expert_of[:], eid[0:1, :])
            v.tensor_scalar(n_items[:], extra_in[0:1, EXPERTS - 1:EXPERTS], float(EXPERTS), None, ALU.add)
            v.wait_ge(tab_full, 1)
            after(v.tensor_scalar(tab_f, tab_ps[:, 0:2 * ITEMS].rearrange("p (a i) -> p a i", a=2), MISSING, 2.0,
                                  ALU.add, ALU.mult))
            v.tensor_copy(w_tab, tab_ps[:, 2 * ITEMS:3 * ITEMS])
            v.tensor_scalar(tab_i, tab_f, K("half"), None, ALU.add).then_inc(tab_ready, 1)

            v.wait_ge(mod_done, 6)
            v.wait_ge(row_in, rows_in(G2))
            for q in range(4):
                r = slice(32 * q, 32 * q + 2)
                last = v.tensor_tensor(mod_row[r, :], mod_ps[r, :], mod_row[r, :], ALU.add)
            last.then_inc(mod_read, 1)

            def x_out(i):
                v.wait_ge(xt_full, i + 1)
                v.tensor_copy(xg_t[:, 4:8, :].rearrange("p a b -> p (a b)"), tp[1][:, :]).then_inc(xt_read_v, 1)

            v.sem_inc(act_ready, 1)
            v.sem_inc(at_read, 1)
            v.sem_inc(y_read_v, 1)
            x_out(0)
            v.wait_ge(tab_ready, 1)
            n = v.value_load(n_items[0:1, 0:1], min_val=EXPERTS, max_val=ITEMS - 1)
            with v.Fori(0, n) as i:
                v.wait_ge(h3_full, i + 1)
                v.wait_ge(sg_ready, i + 1)
                v.wait_ge(at_full, i + 1)
                v.tensor_tensor(act, sg, acc[1][:, 0:256], ALU.mult).then_inc(act_ready, 1)
                x_out(i + 1)
                v.wait_ge(at_full, i + 2)
                v.wait_ge(y_full, i + 1)
                v.tensor_copy(act_t[:, :, :].rearrange("p a b -> p (a b)"), acc[2][:, 0:256]).then_inc(at_read, 1)
                v.wait_ge(y_full, i + 2)
                v.wait_ge(y_free, i + 1)
                v.tensor_scalar(y_sb[:, 1, :], sc_ps[1][:, :], w_tab[:, bass.ds(i, 1)], None, ALU.mult).then_inc(y_read_v, 1)

            v.wait_ge(g2_in, 2 * 16)
            for t in range(TILES):
                y0, y1 = y_in(0, t), y_in(1, t)
                v.wait_ge(yk_in[t], 32)
                after(v.tensor_tensor(y0, y0, y1, ALU.add))
                after(v.tensor_tensor(y0, y0, g2b[:, min(t, 1), :], ALU.mult))
                v.tensor_tensor(x1[:, t, :], x1[:, t, :], y0, ALU.add).then_inc(final_ready, 1)

        @block.gpsimd
        def _(g_):
            g = g_
            own = [0]

            def after(ins):
                own[0] += 1
                ins.then_inc(p_step, 1)
                g.wait_ge(p_step, own[0])

            def load_row(n):
                b = ins["b_mod"][0].rearrange("(g q n) -> g q n", g=6, q=4)[n]
                gn = ins["g_attn" if n < G1 else "g_ffn"][0].rearrange("(q n) -> q n", q=4)
                for c in range(2):
                    g.dma_start(mod_row[c:P:32, :], b).then_inc(row_in, 16)
                    if n in (SC1, SC2):
                        g.dma_start(gain_row[c:P:32, :], gn).then_inc(row_in, 16)

            def store_row(n):
                if n in (SC1, SC2):
                    g.wait_ge(row_scaled, (SC1, SC2).index(n) + 1)
                else:
                    g.wait_ge(mod_read, n + 1)
                for c in range(2):
                    g.dma_start(mod_d[n, c].rearrange("(q n) -> q n", q=4), mod_row[c:P:32, :]).then_inc(row_out, 16)
                g.wait_ge(row_out, 32 * (n + 1))

            def power(dst, src, n):
                return g.tensor_tensor(dst, src, K("pow")[:, 0:n], ALU.pow)

            load_row(SH1)
            g.wait_ge(const_in, 16)
            for t in range(TILES):
                g.wait_ge(ssx_ready, t + 1)
                after(g.tensor_scalar(ssx[:, t:t + 1], ssx[:, t:t + 1], 1.0 / D, EPS, ALU.mult, ALU.add))
                power(rx[:, t:t + 1], ssx[:, t:t + 1], 1).then_inc(rx_ready, 1)
            for s in steps:
                if s[0] == "mod" and s[2] == KD - 1 and s[1] != G2:
                    n = s[1]
                    store_row(n)
                    load_row(n + 1)
                    if n in (SH1, SC1):
                        for c in range(2):
                            g.dma_start(mod_t[:, n, c, :], mod_d[n, c].rearrange("(p k) -> p k", k=KD)).then_inc(modt_in, 16)
                elif s[0] in ("proj", "kvc"):
                    n = s[1]
                    b, kind = n % 2, jobs[n][0]
                    heads, dim = {"ckv": (1, KV_RANK), "cq0": (2, 192), "cq1": (2, 192), "kvc": (2, 192),
                                  "akv": (2, HD), "bkv": (2, HD)}.get(kind, (3, HD))
                    sv = ss[b][:, 0:heads]
                    g.wait_ge(z_ready, n + 1)
                    if kind == "kvc":
                        tt = jobs[n][1]
                        g.wait_ge(krg_ready, (1, 4, 2, 3)[tt])
                        after(g.tensor_scalar(sv, sv, kr_ss[:, tt:tt + 1], 1.0 / dim, ALU.add, ALU.mult))
                    else:
                        after(g.tensor_scalar(sv, sv, 1.0 / dim, EPS, ALU.mult, ALU.add))
                    power(rstd[b][:, 0:heads], sv, heads).then_inc(rstd_ready, 1)
                elif s == ("cache", "a"):
                    g.wait_ge(o_full, 12)
                    for k in "ab":
                        g.dma_start(v_ab[k.upper()][:, 1, :, :], ins[f"cache_{k}_v"][0, 0]).then_inc(cache_v_in, 16)
                elif s[0] == "out":
                    _, cc, t = s
                    if (cc, t) == (0, 0):
                        g.wait_ge(acc_full, n_jobs)
                        g.dma_start(x1[:, 0, :], ins["x_prompt"][0]).then_inc(xres_in, 16)
                        g.dma_start(x1[:, 1:3, :], ins["x_sample"][0].rearrange("(t p) d -> p t d", p=P)).then_inc(xres_in, 16)
                        g.wait_ge(o_ready, n_atts)
                        g.wait_ge(state_out, 6 * 16)
                        for dst, n, done in ((g1b, G1, g1_in), (a2b, SC2, a2_in), (sh2b, SH2, sh2_in)):
                            for c in range(2):
                                g.dma_start(dst[:, c, :], mod_d[n, c].partition_broadcast(P)).then_inc(done, 16)
                        g.dma_start(w_r[:, :, 0:GROUPS], ins["w_rg"][0].rearrange("(p k) n -> p k n", k=KD)).then_inc(wr_in, 16)
                        g.dma_start(w_r[:, :, GROUPS:], ins["w_re"][0].rearrange("(p k) n -> p k n", k=KD)).then_inc(wr_in, 16)
                    if cc == 3:
                        g.wait_ge(ss2s_ready, t + 1)
                        after(g.tensor_scalar(ss2s[:, t:t + 1], ss2s[:, t:t + 1], 1.0 / D, EPS, ALU.mult, ALU.add))
                        power(r2s[:, t:t + 1], ss2s[:, t:t + 1], 1).then_inc(r2_ready, 1)
                        g.wait_ge(h2_ready, t + 1)
                        g.dma_start(h2_d[t * P:(t + 1) * P, :], h2[:, t, :]).then_inc(h2_out, 16)

            h2_rows = h2_d.rearrange("t (h n) -> (t h) n", h=2)
            y_rows = y_d.rearrange("t (h n) -> (t h) n", h=2)

            gather_bound, scatter_bound = g.to_reg(2 * T - 1), g.to_reg(2 * T * TOP_K - 1)

            def gather():
                g.indirect_dma_start(out=xg, out_offset=None, in_=h2_rows,
                                     in_offset=bass.IndirectOffsetOnAxis(ap=gat_now[:], axis=0),
                                     bounds_check=gather_bound, oob_is_err=False).then_inc(xg_in, 16)

            g.sem_inc(y_free, 1)
            g.wait_ge(h2_out, TILES * 16)
            g.wait_ge(tab_ready, 1)
            g.wait_ge(xg_clear, 1)
            after(g.tensor_copy(gat_now[:], tab_i[:, 0, 0:1]))
            gather()
            n = g.value_load(n_items[0:1, 0:1], min_val=EXPERTS, max_val=ITEMS - 1)
            g.wait_ge(mod_read, 6)
            for c in range(2):
                g.dma_start(mod_d[G2, c].rearrange("(q n) -> q n", q=4), mod_row[c:P:32, :]).then_inc(row_out, 16)
            g.wait_ge(row_out, 6 * 32)
            for c in range(2):
                g.dma_start(g2b[:, c, :], mod_d[G2, c].partition_broadcast(P)).then_inc(g2_in, 16)
            with g.Fori(0, n) as i:
                g.wait_ge(xt_full, i + 1)
                g.wait_ge(xg_in, i * 16 + 16)
                g.tensor_copy(gat_now[:], tab_i[:, 0, bass.ds(i + 1, 1)]).then_inc(gidx, 1)
                g.wait_ge(tab_ready, 1)
                g.wait_ge(gidx, i + 1)
                gather()
                g.tensor_copy(sca_now[:], tab_i[:, 1, bass.ds(i, 1)]).then_inc(sidx, 1)
                g.wait_ge(sidx, i + 1)
                g.wait_ge(y_read_a, i + 2)
                g.wait_ge(y_read_v, i + 2)
                g.sem_inc(y_whole, 1)
                g.indirect_dma_start(out=y_rows, out_offset=bass.IndirectOffsetOnAxis(ap=sca_now[:], axis=0),
                                     in_=y_sb[:, :, :].rearrange("p a b -> p (a b)"), in_offset=None,
                                     bounds_check=scatter_bound, oob_is_err=False).then_inc(y_out, 16)
                g.wait_ge(y_out, i * 16 + 16)
                g.sem_inc(y_free, 1)


def kernel(**inputs):
    import concourse.bacc as bacc
    from concourse.bass_utils import run_bass_kernel_spmd as run

    nc = bacc.Bacc("TRN2", target_bir_lowering=False, num_devices=1)
    arrays = {f"in_{n}": np.ascontiguousarray(inputs[n]) for n in IN_NAMES}
    arrays["in_consts"] = constants()
    ins = {n[3:]: nc.dram_tensor(n, a.shape, mybir.dt.from_np(a.dtype), kind="ExternalInput").ap()
           for n, a in arrays.items()}
    outs = {n: nc.dram_tensor(f"out_{n}", s, F32, kind="ExternalOutput").ap() for n, s in OUTS}
    build(nc, ins, outs)
    r = run(nc, [arrays], core_ids=[0])
    return tuple(r.results[0][f"out_{n}"] for n, _ in OUTS)
```

```python
from contextlib import ExitStack

import concourse.bass as bass
import numpy as np
from concourse import mybir

F32 = mybir.dt.float32
I32 = mybir.dt.int32
BF16 = mybir.dt.bfloat16
ACT = mybir.ActivationFunctionType
ALU = mybir.AluOpType
AX = mybir.AxisListType.X

P = 128
D = 2048
TILES = 3
T = TILES * P
KD = D // P
HD = 128
HEADS_A, HEADS_B, HEADS_C = 6, 6, 4
HEADS = HEADS_A + HEADS_B + HEADS_C
ROPE = 64
KV_RANK = 256
GRID_W = 64
EPS = 1e-6
THETA = 10000.0
NEG = -1e30
GROUPS, PER_GROUP = 4, 8
EXPERTS = GROUPS * PER_GROUP
TOP_K = 2
FF = 512
CAP = 64
MAX_Q = T // CAP
ITEMS = EXPERTS + (T * TOP_K - EXPERTS) // CAP + 1
ASSIGN = TOP_K * TILES
MISSING = 4096.0

SLOTS = 12
MOE_UNITS = 12
HALF = D // 2
BACKS = 4 * TILES
FIRST_BACK = 2

Q_A, K_A, V_A = 0, 768, 1024
Q_B, K_B, V_B = 1280, 2048, 2304
Q_C, CKV, KR = 2560, 3328, 3584

CHUNKS = [("ckv", CKV, 320), ("cq0", Q_C, 384), ("cq1", Q_C + 384, 384),
          ("aq0", Q_A, 384), ("aq1", Q_A + 384, 384), ("bq0", Q_B, 384),
          ("akv", K_A, 512), ("bq1", Q_B + 384, 384), ("bkv", K_B, 512)]


SH1, SC1, G1, SH2, SC2, G2 = range(6)


def const_layout():
    at, out = 0, {}
    for name, n in (("ident", P), ("tri", P), ("ones", P), ("mask", 2 * P), ("cos", 2 * 64), ("sin", 2 * 64),
                    ("cosr", 2 * 32), ("sinr", 2 * 32), ("half", 1), ("items", ITEMS), ("slots", P),
                    ("rev32", EXPERTS), ("rev4", GROUPS), ("experts", EXPERTS), ("tok", ASSIGN),
                    ("pow", 4), ("row_of", 8),
                    ("caps", MAX_Q - 1)):
        out[name] = (at, n)
        at += n
    out["tokens"] = (at, T)
    return out, at


def constants():
    lay, n = const_layout()
    c = np.zeros((P, n + T), np.float32)

    def put(name, v):
        at, w = lay[name]
        c[:, at:at + w] = np.asarray(v, np.float32).reshape(-1, w)

    p = np.arange(P)
    put("ident", np.eye(P))
    put("tri", p[:, None] < p[None, :])
    put("ones", np.ones((P, P)))
    put("mask", np.concatenate([np.where(p[None, :] <= p[:, None], 0.0, NEG),
                                np.where(p[:, None] <= p[None, :], 0.0, NEG)], 1))
    tok = np.arange(2 * P)
    for dim, cn, sn in ((HD, "cos", "sin"), (ROPE, "cosr", "sinr")):
        axis = dim // 2
        inv = np.float32(THETA) ** (-np.arange(0, axis, 2, dtype=np.float32) / np.float32(axis))
        row, col = (tok // GRID_W).astype(np.float32), (tok % GRID_W).astype(np.float32)
        ang = np.concatenate([row[:, None] * inv, col[:, None] * inv], 1).astype(np.float32)
        for name, v in ((cn, np.cos(ang)), (sn, np.sin(ang))):
            put(name, v.reshape(2, P, axis).transpose(1, 0, 2).reshape(P, -1))
    put("tokens", np.arange(T)[None])
    put("half", (p // CAP)[:, None])
    put("items", np.arange(ITEMS)[None])
    put("slots", (p % CAP)[None])
    put("rev32", EXPERTS - np.arange(EXPERTS)[None])
    put("rev4", GROUPS - np.arange(GROUPS)[None])
    put("experts", np.arange(EXPERTS)[None])
    t = np.arange(TILES)[None] * P + p[:, None]
    put("tok", np.concatenate([t] * TOP_K, 1) - MISSING)
    put("pow", -0.5 * np.ones((P, 4)))
    put("caps", CAP * np.arange(1, MAX_Q)[None])
    put("row_of", p[:, None] == (32 * (np.arange(8) // 2) + np.arange(8) % 2)[None])
    return c


def plan():
    steps, jobs, atts = [], [], []
    units = []

    def mod(g, k):
        units.append(("mod", g, k))
        steps.append(("mod", g, k))

    for k in range(KD):
        mod(SH1, k)
    for k in range(KD):
        mod(SC1, k)
        if k == 3:
            steps.append(("modt", SH1))
    steps.append(("modt", SC1))
    steps.append(("hmod",))
    later = [(g, k) for g in (G1, SH2, SC2, G2) for k in range(KD)]
    pending = []

    def job(kind, what, norm=True):
        jobs.append(what)
        steps.append((kind, len(jobs) - 1))
        if norm:
            steps.append(("norm", len(jobs) - 1))
        if len(pending) == 2:
            steps.append(("turn", pending.pop(0)))
        pending.append(len(jobs) - 1)

    def kvc(tt, pair):
        job("kvc", ("kvc", tt, pair))

    scored, unnormalised, turned_p = [], [], []

    def advance(u=None):
        if u is not None:
            steps.append(("qk", u))
            scored.append(u)
        if turned_p:
            steps.append(("pv", turned_p.pop()))
        if unnormalised:
            steps.append(("nz", unnormalised.pop()))
        if u is not None:
            unnormalised.append(u)
        if scored and (u is None or len(scored) > 2):
            if unnormalised == [scored[0]]:
                steps.append(("nz", unnormalised.pop()))
            steps.append(("pt", scored[0]))
            turned_p.append(scored.pop(0))

    def attend(group, heads, fill=(), flush=False):
        fill = list(fill)
        for h in heads:
            for t in range(TILES):
                if fill:
                    mod(*fill.pop(0))
                atts.append((group, h, t))
                advance(len(atts) - 1)
        while flush and (scored or turned_p):
            advance()

    kvcs = [(tt, pair) for tt in range(4) for pair in range(2)]
    for name, _, _ in CHUNKS:
        units.extend([("in", name, i) for i in range(4)])
        for t in range(TILES):
            attends = (name == "aq0" and t > 0) or (name == "aq1" and t < 2) or name in ("bq1", "bkv")
            job("proj", (name, t), norm=not attends)
            n = len(jobs) - 1
            if name == "ckv" and t == TILES - 1:
                units.append(("ukv",))
                steps.append(("cache", "c"))
            if name == "cq0" or (name == "ckv" and t == TILES - 1):
                for _ in range(2):
                    job("kvc", ("kvc", *kvcs.pop(0)))
            if name == "akv" and t == 0:
                steps.append(("cache", "a"))
            for g, k in later[:2]:
                mod(g, k)
            del later[:2]
            if name == "aq0" and t:
                attend("C", [t - 1])
            if name == "aq1" and t < 2:
                attend("C", [t + 2], flush=(t == 1))
            if name == "bq1":
                if t == 0:
                    steps.append(("turn", pending.pop(0)))
                attend("A", [2 * t])
            if name == "bkv":
                attend("A", [2 * t + 1])
            if attends:
                steps.append(("norm", n))
    while turned_p:
        advance()
    steps.append(("cache", "b"))
    steps.extend(("turn", n) for n in pending)
    attend("B", range(HEADS_B), fill=later, flush=True)
    for cc in range(4):
        units.extend([("out", cc, i) for i in range(4)])
        for t in range(TILES):
            steps.append(("out", cc, t))
    return steps, jobs, atts, units


IN_NAMES = ["x_prompt", "x_sample", "cache_a_k", "cache_a_v", "cache_b_k", "cache_b_v", "cache_c_kv",
            "cache_c_krope", "c", "c_ctx", "g_attn", "g_ffn", "w_mod", "b_mod", "w_in", "a_qn", "a_kn",
            "b_qn", "b_kn", "b_sink", "c_kvn", "w_ukv", "c_qn", "c_kn", "w_o", "w_rg", "b_rg", "w_re",
            "b_re", "w1", "w3", "w2"]
OUTS = [("y_prompt", (1, P, D)), ("y_sample", (1, 2 * P, D)),
        ("state_a_k", (1, 1, P, 2, HD)), ("state_a_v", (1, 1, P, 2, HD)),
        ("state_b_k", (1, 1, P, 2, HD)), ("state_b_v", (1, 1, P, 2, HD)),
        ("state_c_kv", (1, 1, P, KV_RANK)), ("state_c_krope", (1, 1, P, ROPE))]


def build(nc, ins, outs):
    steps, jobs, atts, units = plan()
    lay, n_const = const_layout()
    chunk_at = {name: (at, w) for name, at, w in CHUNKS}
    unit_no = {u: m for m, u in enumerate(units)}
    n_static = len(units)
    n_jobs, n_atts = len(jobs), len(atts)

    key_tile = [0, 2, 3]

    tp_no, n_tp = {}, KD
    last_turn, turn_before = n_tp, {}
    output_in = {}
    for s in steps:
        if s[0] in ("turn", "cache", "pt"):
            tp_no[s] = n_tp
            if s[0] == "pt":
                output_in[n_tp] = s[1]
            n_tp += 1
            if s[0] != "pt":
                last_turn = n_tp
        if s[0] == "qk":
            turn_before[s[1]] = last_turn
    groups_order = [SH1, SC1, G1, SH2, SC2, G2]

    def attention_of(u):
        g, h, t = atts[u]
        keys = slice(0, P) if t == 0 else slice(P, 4 * P)
        tiles = [0] if t == 0 else [1, 2, 3]
        return g, h, t, keys, tiles

    with ExitStack() as ctx:
        def sb(name, shape, dt=F32):
            return ctx.enter_context(nc.sbuf_tensor(name, shape, dt))

        def sem(name):
            return ctx.enter_context(nc.semaphore(name))

        ring = sb("ring", [P, SLOTS, D])
        r1 = sb("r1", [P, TILES * D])
        r2 = sb("r2", [P, TILES * D])
        r3 = sb("r3", [P, 6 * D + 192])
        cst = sb("cst", [P, n_const])
        gains = sb("gains", [P, 1200])
        csil = sb("csil", [P, KD, 2])
        cvec = sb("cvec", [P, 2, KD])
        mod_row = sb("mod_row", [P, 512])
        gain_row = sb("gain_row", [P, 512])
        mod_t = sb("mod_t", [P, 2, 4, 8])
        small = sb("small", [P, 80])
        n_items = sb("n_items", [1, 1], I32)
        expert_of = sb("expert_of", [1, ITEMS], I32)
        gat_now = sb("gat_now", [P, 1], I32)

        def K(name):
            at, w = lay[name]
            return cst[:, at:at + w]

        ident, tri, ones = K("ident"), K("tri"), K("ones")
        h_t = r1[:].rearrange("p (k t) -> p k t", k=KD)
        x1 = r1[:].rearrange("p (t d) -> p t d", t=TILES)
        xn = r2[:].rearrange("p (t d) -> p t d", t=TILES)
        qo = r2[:].rearrange("p (t h q) -> p t h q", t=TILES, h=HEADS)
        h2 = xn
        y_sum = xn

        at3 = [0]

        def r3_at(at, *shape):
            n = int(np.prod(shape))
            v = r3[:, at:at + n]
            names = "abcd"[:len(shape)]
            return v.rearrange(f"p ({' '.join(names)}) -> p {' '.join(names)}",
                               **dict(zip(names[:-1], shape[:-1])))

        def r3_next(*shape):
            v = r3_at(at3[0], *shape)
            at3[0] += int(np.prod(shape))
            assert at3[0] <= 6 * D + 192
            return v

        k_c, v_c = r3_at(0, 4, 4 * P), r3_at(2048, 4, 4, HD)
        k_ab = {"A": r3_at(0, 2, 4 * P), "B": r3_at(2048, 2, 4 * P)}
        v_ab = {"A": r3_at(1024, 4, 2, HD), "B": r3_at(3072, 4, 2, HD)}
        at3[0] = 4096
        kr_c, qr_c = r3_next(2, 4 * P), r3_next(2, T)
        ckv_t = r3_next(2, 4 * P)
        zt = [r3_next(512) for _ in range(3)]
        junk = r3_next(384)
        rope_tmp = r3_next(4, 192)
        prob = [r3_next(384), r3_next(384)]
        prob_t = [r3_next(3, P), r3_next(3, P)]
        kr, krg = r3_next(4, ROPE), r3_next(4, ROPE)
        junk_c = r3_next(ROPE)
        cached = {"c": r3_next(2 * P), "a": r3_next(2 * P), "b": r3_next(2 * P)}
        g1b, sh2b, a2b = (r3_at(i * 2 * D, 2, D) for i in range(3))
        h2_t = [r3_at(at, KD, P) for at in (4 * D, 2 * D, 0)]
        g2b = r3_at(0, 2, D)
        xg, xg_t = r3_at(4096, HALF), r3_at(5120, 8, P)
        at3[0] = 6144
        lg = r3_next(TILES, GROUPS + EXPERTS)
        g_s, g_eq, g_oh, g_pen = (r3_next(TILES, GROUPS) for _ in range(4))
        sel, e_eq = r3_next(TILES, EXPERTS), r3_next(TILES, EXPERTS)
        oh = r3_next(ASSIGN, EXPERTS)
        oh_before = r3_next(ASSIGN + 1, EXPERTS)
        oh_tmp = r3_next(ASSIGN, EXPERTS)
        extra, extra_in, extra_ex, zero32 = (r3_next(EXPERTS) for _ in range(4))
        at_item = r3_next(ASSIGN, ITEMS)
        at_slot = r3_next(ASSIGN, P)
        vals = r3_next(ASSIGN, 2, ITEMS)
        vals_end = at3[0]
        tok_tab, row_f = r3_next(ITEMS), r3_next(ITEMS)
        row_tab = r3_next(ITEMS).bitcast(I32)
        w_tab = r3_next(ITEMS)
        over = r3_next(ITEMS - EXPERTS, EXPERTS)
        beyond = r3_next(EXPERTS, MAX_Q - 1)
        eid = r3_next(ITEMS)
        asg = r3_next(12, ASSIGN)
        tri3 = r3_next(12, TILES)
        sg, act = r3_next(256), r3_next(256)
        act_t = r3_next(2, P)
        y_sb = r3_next(2, 512)
        y_part = r3_at(6144, 3, 2, 256).bitcast(BF16)
        of_token = r3_at(6144 + 1536, T // 2).bitcast(BF16)
        assert 6144 + 1536 + T // 2 <= vals_end
        tokens = r3_next(T)

        off = [0]

        def gain(n):
            v = gains[:, off[0]:off[0] + n]
            off[0] += n
            return v

        gain_of = {n: gain(w) for n, w in (("a_qn", HD), ("a_kn", HD), ("b_qn", HD), ("b_kn", HD),
                                           ("c_kvn", KV_RANK), ("c_qn", 192), ("c_kn", 192))}
        sink = gain(HEADS_B)
        r_bias = gain(GROUPS + EXPERTS)
        junk2 = gains[:, 0:512]
        w_r = gains[:, 512:512 + KD * 36].rearrange("p (k n) -> p k n", k=KD)

        s_at = [0]

        def sm(n):
            v = small[:, s_at[0]:s_at[0] + n]
            s_at[0] += n
            return v

        ss, rstd = ([sm(4) for _ in range(3)] for _ in range(2))
        kr_ss = sm(4)
        mx, nmx, rsum, rinv, esink = ([sm(1), sm(1)] for _ in range(5))
        ssx, rx = sm(4), sm(4)
        ss2 = sm(12)
        ss2s, r2s = sm(4), sm(4)

        bank = [ctx.enter_context(nc.psum_tensor(f"bank{i}", [P, 512], F32)) for i in range(8)]
        acc, mod_ps, tp, sc_ps = bank[0:3], bank[3], bank[4:6], bank[6:8]
        n_acc = n_jobs + 4 * TILES
        lg_ps, rank_ps, tab_ps = (acc[(n_acc + i) % 3] for i in range(3))

        mod_d = nc.dram_tensor("mod_d", [6, 2, D], F32).ap()
        h2_d = nc.dram_tensor("h2_d", [T, D], F32).ap()

        slot_full = [sem(f"slot_full{i}") for i in range(SLOTS)]
        slot_free = [sem(f"slot_free{i}") for i in range(SLOTS)]
        cond_in, x_in, const_in, gains_in = sem("cond_in"), sem("x_in"), sem("const_in"), sem("gains_in")
        cache_k_in, cache_v_in = sem("cache_k_in"), sem("cache_v_in")
        cleared, csil_ready = sem("cleared"), sem("csil_ready")
        row_in, mod_done, mod_read, row_scaled, row_out = (sem(n) for n in (
            "row_in", "mod_done", "mod_read", "row_scaled", "row_out"))
        modt_full, modt_ready = sem("modt_full"), sem("modt_ready")
        ssx_ready, rx_ready, xn_ready = sem("ssx_ready"), sem("rx_ready"), sem("xn_ready")
        tp_full, tp_read = sem("tp_full"), sem("tp_read")
        h_ready = sem("h_ready")
        acc_full = sem("acc_full")
        z_ready, rstd_ready, norm_ready, turned = (sem(n) for n in ("z_ready", "rstd_ready", "norm_ready", "turned"))
        krg_ready, krss_ready = sem("krg_ready"), sem("krss_ready")
        state_out = sem("state_out")
        s_full, nmax_ready, e_ready, p_ready, o_full, o_ready = (sem(n) for n in (
            "s_full", "nmax_ready", "e_ready", "p_ready", "o_full", "o_ready"))
        g1_in, sh2_in, a2_in, xres_in, wr_in = (sem(n) for n in ("g1_in", "sh2_in", "a2_in", "xres_in", "wr_in"))
        x1_ready, ss2_ready, ss2s_ready, r2_ready, h2_ready, h2_out = (sem(n) for n in (
            "x1_ready", "ss2_ready", "ss2s_ready", "r2_ready", "h2_ready", "h2_out"))
        ht_full, ht_read_a, ht_read_v = sem("ht_full"), sem("ht_read_a"), sem("ht_read_v")
        lg_full = sem("lg_full")
        ge_in, ge_out, re_in, re_out = sem("ge_in"), sem("ge_out"), sem("re_in"), sem("re_out")
        oh_ready, rank_full, vals_ready, tab_full, tab_ready = (sem(n) for n in (
            "oh_ready", "rank_full", "vals_ready", "tab_full", "tab_ready"))
        gidx, xg_in, xt_full, xt_read_a, xt_read_v = (sem(n) for n in (
            "gidx", "xg_in", "xt_full", "xt_read_a", "xt_read_v"))
        xg_clear = sem("xg_clear")
        h1_full, h3_full, sg_ready, act_ready, at_full, at_read = (sem(n) for n in (
            "h1_full", "h3_full", "sg_ready", "act_ready", "at_full", "at_read"))
        y_full, y_read_a, y_read_v = sem("y_full"), sem("y_read_a"), sem("y_read_v")
        tokens_in, y_split, back_full, back_read = (sem(n) for n in ("tokens_in", "y_split", "back_full", "back_read"))
        sum_clear, sum_ready = sem("sum_clear"), sem("sum_ready")
        y_upper, y_rest, y_middle = sem("y_upper"), sem("y_rest"), sem("y_middle")
        g2_in, final_ready, final_ready_p, final_out = (sem(n) for n in ("g2_in", "final_ready", "final_ready_p", "final_out"))
        v_step, p_step = sem("v_step"), sem("p_step")

        block = ctx.enter_context(nc.Block())

        def rows_in(n):
            return 32 * (n + 1 + (n >= SC1) + (n >= SC2))

        def unit_source(u, e=0):
            kind = u[0]
            if kind == "mod":
                _, g, k = u
                return (ins["w_mod"][0].rearrange("(p j) n -> p j n", j=KD)[:, k, g * D:(g + 1) * D], (D,))
            if kind == "in":
                _, name, i = u
                at, w = chunk_at[name]
                return (ins["w_in"][0].rearrange("(j p) n -> p j n", p=P)[:, 4 * i:4 * i + 4, at:at + w], (4, w))
            if kind == "ukv":
                return ins["w_ukv"][0].rearrange("(j p) n -> p j n", j=2), (2, 1024)
            if kind == "out":
                _, cc, i = u
                return (ins["w_o"][0].rearrange("(j p) n -> p j n", p=P)[:, 4 * i:4 * i + 4, cc * 512:(cc + 1) * 512],
                        (4, 512))
            _, n = u
            if n < 8:
                w = ins["w1" if n < 4 else "w3"][0][bass.ds(e, 1)]
                half, j = (n % 4) // 2, 4 * (n % 2)
                return (w.rearrange("e (h p j) n -> h p (e j) n", h=2, j=8)[half][:, j:j + 4, :], (4, 512))
            w = ins["w2"][0][bass.ds(e, 1)]
            return w.rearrange("e (j p) n -> j p (e n)", p=P)[n - 8], (D,)

        def cut(slot, shape):
            v = ring[:, slot, 0:int(np.prod(shape))]
            return v if len(shape) == 1 else v.rearrange("p (a b) -> p a b", a=shape[0])

        frees, acc_uses, slot_uses = {}, 0, [0] * SLOTS
        for s in steps:
            if s[0] == "mod":
                m = unit_no[("mod", s[1], s[2])]
                if s[2] == KD - 1:
                    frees[m] = (mod_done, groups_order.index(s[1]) + 1)
                    continue
                done = [m]
            elif s[0] in ("proj", "kvc", "out"):
                acc_uses += 1
                last = False
                if s[0] == "proj" and jobs[s[1]][1] == TILES - 1:
                    own, last = [unit_no[("in", jobs[s[1]][0], i)] for i in range(4)], True
                elif s[0] == "out" and s[2] == TILES - 1:
                    own, last = [unit_no[("out", s[1], i)] for i in range(4)], True
                elif s[0] == "kvc" and jobs[s[1]][1:] == (3, 1):
                    own, last = [unit_no[("ukv",)]], True
                if not last:
                    continue
                frees[own[-1]] = (acc_full, acc_uses)
                done = own[:-1]
            else:
                continue
            for m in done:
                slot_uses[m % SLOTS] += 1
                frees[m] = (slot_free[m % SLOTS], slot_uses[m % SLOTS])
        assert sorted(frees) == list(range(n_static))
        moe_done = {3: h1_full, 7: h3_full, 11: y_full}

        @block.sync
        def _(sp):
            for m, u in enumerate(units):
                slot = m % SLOTS
                if m >= SLOTS:
                    sp.wait_ge(*frees[m - SLOTS])
                src, shape = unit_source(u)
                sp.dma_start(cut(slot, shape), src).then_inc(slot_full[slot], 16)

            for u in range(MOE_UNITS):
                slot = (n_static + u) % SLOTS
                sp.wait_ge(*frees[n_static + u - SLOTS])
                src, shape = unit_source(("moe", u), 0)
                sp.dma_start(cut(slot, shape), src).then_inc(slot_full[slot], 16)
            sp.wait_ge(tab_ready, 1)
            n = sp.value_load(n_items[0:1, 0:1], min_val=EXPERTS, max_val=ITEMS - 1)
            with sp.Fori(1, n) as i:
                e = sp.value_load(expert_of[0:1, bass.ds(i, 1)], min_val=0, max_val=EXPERTS - 1)
                for u in range(MOE_UNITS):
                    slot = (n_static + u) % SLOTS
                    if u in moe_done:
                        sp.wait_ge(moe_done[u], i + (1 if u == 11 else 0))
                    else:
                        sp.wait_ge(slot_free[slot], i + slot_uses[slot])
                    src, shape = unit_source(("moe", u), e)
                    sp.dma_start(cut(slot, shape), src).then_inc(slot_full[slot], 16)

            for t in range(TILES):
                sp.wait_ge(*((final_ready_p, 1) if t == 0 else (final_ready, t)))
                dst = outs["y_prompt"][0] if t == 0 else outs["y_sample"][0, (t - 1) * P:t * P, :]
                sp.dma_start(dst, x1[:, t, :]).then_inc(final_out, 16)
            sp.wait_ge(final_out, 16 * TILES)

        @block.tensor
        def _(pe):
            def arrived(m):
                pe.wait_ge(slot_full[m % SLOTS], (m // SLOTS + 1) * 16)

            pe.wait_ge(const_in, 16)
            pe.wait_ge(xn_ready, TILES)
            for k in range(KD):
                if k >= 2:
                    pe.wait_ge(tp_read, k - 1)
                for t in range(TILES):
                    mm = pe.transpose(tp[k % 2][:, t * P:(t + 1) * P], xn[:, t, k * P:(k + 1) * P], ident)
                mm.then_inc(tp_full, 1)

            pe.wait_ge(csil_ready, 1)
            pe.wait_ge(cleared, 1)

            def mod_step(g, k):
                m = unit_no[("mod", g, k)]
                arrived(m)
                n = groups_order.index(g)
                if k == 0 and n:
                    pe.wait_ge(mod_read, n)
                for q in range(4):
                    mm = pe.matmul(mod_ps[32 * q:32 * q + 2, :], csil[:, k, :], ring[:, m % SLOTS, q * 512:(q + 1) * 512],
                                   start=(k == 0), stop=(k == KD - 1))
                mm.then_inc(*((slot_free[m % SLOTS], 1) if k < KD - 1 else (mod_done, 1)))

            def acc_wait(a):
                if 3 <= a < n_jobs + 3:
                    pe.wait_ge(z_ready, a - 2)
                elif a >= n_jobs + 3:
                    pe.wait_ge(x1_ready, a - 2 - n_jobs)

            def tp_bank(s):
                n = tp_no[s]
                pe.wait_ge(tp_read, n - 1)
                if n - 2 in output_in:
                    pe.wait_ge(o_ready, output_in[n - 2] + 1)
                return tp[n % 2]

            def turn_h2(t):
                pe.wait_ge(h2_ready, t + 1)
                for b in range(4):
                    if t:
                        pe.wait_ge(*((ht_read_a, 2 * t - 1 + b // 2) if b % 2 == 0 else (ht_read_v, 2 * t - 1 + b // 2)))
                    for i in range(4):
                        mm = pe.transpose(bank[4 + b][:, i * P:(i + 1) * P], h2[:, t, 4 * b + i::KD], ident)
                    mm.then_inc(ht_full, 1)

            def logits(t):
                pe.wait_ge(wr_in, 2 * 16)
                pe.wait_ge(ht_read_a, 2 * t + 2)
                pe.wait_ge(ht_read_v, 2 * t + 2)
                for k in range(KD):
                    mm = pe.matmul(lg_ps[:, t * 36:(t + 1) * 36], h2_t[t][:, k, :], w_r[:, k, :],
                                   start=(k == 0), stop=(k == KD - 1))
                if t == TILES - 1:
                    mm.then_inc(lg_full, 1)

            def router(t):
                if t == 0:
                    acc_wait(n_jobs + 4 * TILES)
                    pe.wait_ge(tp_read, n_tp)
                turn_h2(t)
                logits(t)

            a = 0
            for s in steps:
                if s[0] == "mod":
                    mod_step(s[1], s[2])
                elif s[0] == "modt":
                    n = s[1]
                    if n == SH1:
                        pe.wait_ge(mod_read, 1)
                    else:
                        pe.wait_ge(row_scaled, 1)
                    for b in range(4):
                        mm = pe.matmul(sc_ps[0][:, 32 * n + 8 * b:32 * n + 8 * b + 8], mod_row[:, b * P:(b + 1) * P],
                                       K("row_of"), start=True, stop=True)
                    mm.then_inc(modt_full, 1)
                elif s[0] == "proj":
                    name, t = jobs[s[1]]
                    w = chunk_at[name][1]
                    acc_wait(a)
                    for i in range(4):
                        m = unit_no[("in", name, i)]
                        arrived(m)
                        wu = cut(m % SLOTS, (4, w))
                        for j in range(4):
                            k = 4 * i + j
                            if a == 0:
                                pe.wait_ge(h_ready, k + 1)
                            mm = pe.matmul(acc[a % 3][:, 0:w], h_t[:, k, t * P:(t + 1) * P], wu[:, j, :],
                                           start=(k == 0), stop=(k == KD - 1))
                        if i == 3:
                            mm.then_inc(acc_full, 1)
                        elif t == TILES - 1:
                            mm.then_inc(slot_free[m % SLOTS], 1)
                    a += 1
                elif s[0] == "kvc":
                    _, tt, pair = jobs[s[1]]
                    acc_wait(a)
                    m = unit_no[("ukv",)]
                    arrived(m)
                    if tt == 1:
                        pe.wait_ge(tp_read, tp_no[("cache", "c")] + 1)
                    elif pair == 0:
                        t_job = jobs.index(("ckv", (0, None, 1, 2)[tt]))
                        pe.wait_ge(tp_read, tp_no[("turn", t_job)] + 1)
                    wu = cut(m % SLOTS, (2, 1024))
                    for j in range(2):
                        mm = pe.matmul(acc[a % 3][:, 0:512], ckv_t[:, j, tt * P:(tt + 1) * P],
                                       wu[:, j, pair * 512:(pair + 1) * 512], start=(j == 0), stop=(j == 1))
                    mm.then_inc(acc_full, 1)
                    a += 1
                elif s[0] == "turn":
                    n = s[1]
                    kind, z = jobs[n][0], zt[n % 3]
                    bankv = tp_bank(s)
                    pe.wait_ge(norm_ready, n + 1)
                    if kind in ("aq0", "aq1", "bq0", "bq1"):
                        cols = [0, P, 2 * P]
                    elif kind in ("cq0", "cq1"):
                        cols = [0, 192, 384]
                    elif kind == "kvc":
                        cols = [0, P, 2 * P]
                    else:
                        cols = [0, P]
                    for i, c in enumerate(cols):
                        mm = pe.transpose(bankv[:, i * P:(i + 1) * P], z[:, c:c + P], ident)
                    mm.then_inc(tp_full, 1)
                elif s[0] == "cache":
                    bankv = tp_bank(s)
                    pe.wait_ge(cache_k_in, 4 * 16)
                    for i in range(2):
                        mm = pe.transpose(bankv[:, i * P:(i + 1) * P], cached[s[1]][:, i * P:(i + 1) * P], ident)
                    mm.then_inc(tp_full, 1)
                elif s[0] == "qk":
                    u = s[1]
                    g, h, t, keys, _ = attention_of(u)
                    nk = keys.stop - keys.start
                    if u >= 2:
                        pe.wait_ge(e_ready, u - 1)
                    elif u == 0:
                        pe.wait_ge(modt_ready, 2)
                    pe.wait_ge(tp_read, turn_before[u])
                    out = sc_ps[u % 2][:, 0:nk]
                    if g == "C":
                        pe.matmul(out, qo[:, t, 12 + h, :], k_c[:, h, keys], start=True, stop=False)
                        lo = 64 * (h % 2)
                        mm = pe.matmul(out, qr_c[lo:lo + 64, h // 2, t * P:(t + 1) * P],
                                       kr_c[lo:lo + 64, h // 2, keys], start=False, stop=True)
                    else:
                        hh = h + (HEADS_A if g == "B" else 0)
                        mm = pe.matmul(out, qo[:, t, hh, :], k_ab[g][:, h // 3, keys], start=True, stop=True)
                    mm.then_inc(s_full, 1)
                elif s[0] == "pt":
                    u = s[1]
                    _, _, _, _, tiles = attention_of(u)
                    bankv = tp_bank(s)
                    pe.wait_ge(p_ready, u + 1)
                    for i in range(len(tiles)):
                        mm = pe.transpose(bankv[:, i * P:(i + 1) * P], prob[u % 2][:, i * P:(i + 1) * P], ident)
                    mm.then_inc(tp_full, 1)
                elif s[0] == "pv":
                    u = s[1]
                    g, h, t, _, tiles = attention_of(u)
                    pe.wait_ge(tp_read, tp_no[("pt", u)] + 1)
                    if g != "C":
                        pe.wait_ge(cache_v_in, 2 * 16)
                    out = tp[tp_no[("pt", u)] % 2][:, 384:512]
                    for i, tt in enumerate(tiles):
                        v = v_c[:, tt, h, :] if g == "C" else v_ab[g][:, tt, h // 3, :]
                        mm = pe.matmul(out, v, prob_t[u % 2][:, i, :],
                                       start=(i == 0), stop=(i == len(tiles) - 1))
                    mm.then_inc(o_full, 1)
                elif s[0] == "out":
                    _, cc, t = s
                    acc_wait(a)
                    if cc == 0 and t == 0:
                        pe.wait_ge(o_ready, n_atts)
                    for i in range(4):
                        m = unit_no[("out", cc, i)]
                        arrived(m)
                        wu = cut(m % SLOTS, (4, 512))
                        for j in range(4):
                            k = 4 * i + j
                            mm = pe.matmul(acc[a % 3][:, :], qo[:, t, k, :], wu[:, j, :],
                                           start=(k == 0), stop=(k == KD - 1))
                        if i == 3:
                            mm.then_inc(acc_full, 1)
                        elif t == TILES - 1:
                            mm.then_inc(slot_free[m % SLOTS], 1)
                    a += 1
                    if cc == 3 and t:
                        router(t - 1)

            router(TILES - 1)

            pe.wait_ge(oh_ready, 1)
            pe.wait_ge(x1_ready, 12)
            pe.matmul(rank_ps[:, 0:192], tri, oh[:, :, :].rearrange("p a e -> p (a e)"), start=True, stop=False)
            pe.matmul(rank_ps[:, 0:192], ones, oh_before[:, 0:ASSIGN, :].rearrange("p a e -> p (a e)"),
                      start=False, stop=True)
            pe.matmul(rank_ps[:, 192:224], ones, oh_before[:, ASSIGN, :], start=True, stop=True).then_inc(rank_full, 1)

            pe.wait_ge(vals_ready, 1)
            for c in range(ASSIGN):
                mm = pe.matmul(tab_ps[:, 0:2 * ITEMS], at_slot[:, c, :], vals[:, c, :, :].rearrange("p v i -> p (v i)"),
                               start=(c == 0), stop=(c == ASSIGN - 1))
            mm.then_inc(tab_full, 1)

            def turn_x():
                for b in range(2):
                    for i in range(4):
                        mm = pe.transpose(tp[b][:, i * P:(i + 1) * P], xg[:, 4 * b + i::8], ident)
                mm.then_inc(xt_full, 1)

            def back(i, k):
                pe.wait_ge(back_read, i * BACKS + k + 1)
                t, c, ct = k // 4, k // 2 % 2, k % 2
                r = slice(64 * ct, 64 * ct + 64)
                for n_part in range(3):
                    mm = pe.matmul((mod_ps, acc[2])[ct][:, :], of_token[r, t * P:(t + 1) * P], y_part[r, n_part, c, :],
                                   start=(n_part == 0), stop=(n_part == 2))
                mm.then_inc(back_full, 1)

            pe.sem_inc(at_full, 1)
            pe.sem_inc(y_full, 1)
            pe.wait_ge(xg_in, 16)
            turn_x()
            pe.wait_ge(tab_ready, 1)
            n = pe.value_load(n_items[0:1, 0:1], min_val=EXPERTS, max_val=ITEMS - 1)
            with pe.Fori(0, n) as i:
                pe.wait_ge(xt_read_a, i + 1)
                pe.wait_ge(xt_read_v, i + 1)
                pe.wait_ge(act_ready, i + 1)
                for w, (ps, full) in enumerate(((acc[0], h1_full), (acc[1], h3_full))):
                    for uu in range(4):
                        u = 4 * w + uu
                        m = n_static + u
                        slot = m % SLOTS
                        pe.wait_ge(slot_full[slot], (i + m // SLOTS + 1) * 16)
                        half = uu // 2
                        for jj in range(4):
                            if jj == 2 and u == FIRST_BACK:
                                pe.wait_ge(y_split, i + 1)
                                pe.wait_ge(at_read, i + 1)
                            if jj == 2 and u >= FIRST_BACK:
                                back(i, 2 * (u - FIRST_BACK))
                            j = 4 * (uu % 2) + jj
                            for ct in range(2):
                                mm = pe.matmul(ps[64 * ct:64 * ct + 64, 0:256], xg_t[:, j, half * 64:half * 64 + 64],
                                               cut(slot, (4, 512))[:, jj, ct * 256:(ct + 1) * 256],
                                               start=(uu == 0 and jj == 0), stop=(uu == 3 and jj == 3))
                        mm.then_inc(full if uu == 3 else slot_free[slot], 1)
                        if u >= FIRST_BACK:
                            back(i, 2 * (u - FIRST_BACK) + 1)
                pe.wait_ge(xg_in, i * 16 + 32)
                turn_x()
                pe.wait_ge(act_ready, i + 2)
                pe.wait_ge(back_read, i * BACKS + BACKS + 2)
                for q in range(2):
                    mm = pe.transpose(acc[2][:, q * P:(q + 1) * P], act[:, q * P:(q + 1) * P], ident)
                mm.then_inc(at_full, 1)
                pe.wait_ge(at_read, i + 2)
                pe.wait_ge(y_read_a, i + 1)
                pe.wait_ge(y_read_v, i + 1)
                for ft in range(4):
                    m = n_static + 8 + ft
                    slot = m % SLOTS
                    pe.wait_ge(slot_full[slot], (i + m // SLOTS + 1) * 16)
                    half, q = ft // 2, ft % 2
                    for c in range(2):
                        for ct in range(2):
                            mm = pe.matmul(sc_ps[c][64 * ct:64 * ct + 64, :], act_t[:, q, half * 64:half * 64 + 64],
                                           ring[:, slot, ct * HALF + c * 512:ct * HALF + (c + 1) * 512],
                                           start=(ft == 0), stop=(ft == 3))
                    mm.then_inc(y_full if ft == 3 else slot_free[slot], 1)

            pe.wait_ge(y_split, n + 1)
            pe.wait_ge(at_read, n + 1)
            for k in range(BACKS):
                back(n, k)

        @block.scalar
        def _(act_e):
            e = act_e
            e.dma_start(cvec[:, 0, :], ins["c_ctx"].rearrange("(p k) -> p k", k=KD)).then_inc(cond_in, 16)
            e.dma_start(cvec[:, 1, :], ins["c"][0].rearrange("(p k) -> p k", k=KD)).then_inc(cond_in, 16)
            e.dma_start(xn[:, 0, :], ins["x_prompt"][0]).then_inc(x_in, 16)
            e.dma_start(xn[:, 1:3, :], ins["x_sample"][0].rearrange("(t p) d -> p t d", p=P)).then_inc(x_in, 16)
            e.dma_start(cst[:], ins["consts"][:, 0:n_const]).then_inc(const_in, 16)
            for name, v in gain_of.items():
                e.dma_start(v, ins[name][0].partition_broadcast(P)).then_inc(gains_in, 16)
            e.dma_start(sink, ins["b_sink"][0].partition_broadcast(P)).then_inc(gains_in, 16)
            e.dma_start(r_bias[:, 0:GROUPS], ins["b_rg"][0].partition_broadcast(P)).then_inc(gains_in, 16)
            e.dma_start(r_bias[:, GROUPS:], ins["b_re"][0].partition_broadcast(P)).then_inc(gains_in, 16)
            e.dma_start(cached["c"], ins["cache_c_kv"][0, 0]).then_inc(cache_k_in, 16)
            e.dma_start(kr[:, 1, :], ins["cache_c_krope"][0, 0]).then_inc(cache_k_in, 16)
            e.dma_start(cached["a"], ins["cache_a_k"][0, 0].rearrange("t h d -> t (h d)")).then_inc(cache_k_in, 16)
            e.dma_start(cached["b"], ins["cache_b_k"][0, 0].rearrange("t h d -> t (h d)")).then_inc(cache_k_in, 16)

            e.wait_ge(cond_in, 32)
            for c in range(2):
                e.activation(csil[:, :, c], cvec[:, c, :], ACT.Silu).then_inc(csil_ready, 1)

            e.wait_ge(x_in, 32)
            for t in range(TILES):
                e.activation(x1[:, t, :], xn[:, t, :], ACT.Square, accum_out=ssx[:, t:t + 1]).then_inc(ssx_ready, 1)
            e.wait_ge(ssx_ready, TILES)
            for k in range(KD):
                e.wait_ge(tp_full, k + 1)
                e.activation(h_t[:, k, :], tp[k % 2][:, 0:T], ACT.Copy).then_inc(tp_read, 1)

            def h2_turned(t):
                for b in (0, 2):
                    e.wait_ge(ht_full, 4 * t + b + 1)
                    e.activation(h2_t[t][:, 4 * b:4 * b + 4, :].rearrange("p a b -> p (a b)"), bank[4 + b][:, :],
                                 ACT.Copy).then_inc(ht_read_a, 1)

            states = 0
            a = 0
            for s in steps:
                if s[0] in ("proj", "kvc"):
                    n = s[1]
                    kind, z, ps = jobs[n][0], zt[n % 3], acc[a % 3]
                    e.wait_ge(acc_full, a + 1)
                    if n:
                        e.wait_ge(z_ready, n)
                    if n >= 3:
                        e.wait_ge(tp_full, tp_no[("turn", n - 3)] + 1)
                    if states:
                        e.wait_ge(state_out, 16 * states)
                    if kind in ("aq0", "aq1", "bq0", "bq1"):
                        heads, w = 3, HD
                    elif kind in ("cq0", "cq1"):
                        heads, w = 2, 192
                    elif kind == "kvc":
                        heads, w = 2, HD
                    elif kind == "ckv":
                        heads, w = 1, KV_RANK
                    else:
                        heads, w = 2, HD
                    step = 256 if kind == "kvc" else w
                    for i in range(heads):
                        e.activation(junk[:, i * w:(i + 1) * w],
                                     ps[:, i * step:i * step + w], ACT.Square,
                                     accum_out=ss[n % 3][:, i:i + 1])
                    if kind in ("akv", "bkv"):
                        g, t = kind[0].upper(), jobs[n][1]
                        if t == 0:
                            e.wait_ge(o_full, 12)
                        e.activation(v_ab[g][:, key_tile[t], :, :].rearrange("p h d -> p (h d)"), ps[:, 256:512], ACT.Copy)
                        last = e.activation(z[:, 0:256], ps[:, 0:256], ACT.Copy)
                    elif kind == "kvc":
                        _, tt, pair = jobs[n]
                        pv = ps[:, :].rearrange("p (h x) -> p h x", h=2)
                        e.activation(v_c[:, tt, 2 * pair:2 * pair + 2, :], pv[:, :, HD:], ACT.Copy)
                        last = e.activation(z[:, 0:256].rearrange("p (h x) -> p h x", h=2), pv[:, :, 0:HD], ACT.Copy)
                    elif kind == "ckv":
                        kt = key_tile[jobs[n][1]]
                        e.activation(junk[:, 256:320], ps[:, 256:320], ACT.Square, accum_out=kr_ss[:, kt:kt + 1])
                        e.activation(kr[:, kt, :], ps[:, 256:320], ACT.Copy)
                        last = e.activation(z[:, 0:256], ps[:, 0:256], ACT.Copy)
                    else:
                        last = e.activation(z[:, 0:384], ps[:, 0:384], ACT.Copy)
                    last.then_inc(z_ready, 1)
                    a += 1
                elif s[0] in ("turn", "cache"):
                    no = tp_no[s]
                    ps = tp[no % 2]
                    if s[0] == "turn":
                        n = s[1]
                        kind = jobs[n][0]
                        if kind in ("ckv", "akv", "bkv") and jobs[n][1] == 0:
                            e.wait_ge(norm_ready, n + 1)
                            if kind == "ckv":
                                e.dma_start(outs["state_c_kv"][0, 0], zt[n % 3][:, 0:256]).then_inc(state_out, 16)
                                e.dma_start(outs["state_c_krope"][0, 0], kr[:, 0, :]).then_inc(state_out, 16)
                            else:
                                g = kind[0]
                                e.dma_start(outs[f"state_{g}_k"][0, 0].rearrange("t h d -> t (h d)"),
                                            zt[n % 3][:, 0:256]).then_inc(state_out, 16)
                                e.dma_start(outs[f"state_{g}_v"][0, 0],
                                            v_ab[g.upper()][:, 0, :, :]).then_inc(state_out, 16)
                            states += 2
                    e.wait_ge(tp_full, no + 1)
                    if s[0] == "cache":
                        if s[1] == "c":
                            e.activation(junk_c, kr[:, 1, :], ACT.Square, accum_out=kr_ss[:, 1:2]).then_inc(krss_ready, 1)
                            dst = ckv_t[:, :, P:2 * P]
                        else:
                            dst = k_ab[s[1].upper()][:, :, P:2 * P]
                        last = e.activation(dst, ps[:, 0:256].rearrange("p (h x) -> p h x", h=2), ACT.Copy)
                    elif kind in ("aq0", "aq1", "bq0", "bq1"):
                        t = jobs[n][1]
                        h0 = {"aq0": 0, "aq1": 3, "bq0": 6, "bq1": 9}[kind]
                        last = e.activation(qo[:, t, h0:h0 + 3, :].rearrange("p h x -> p (h x)"), ps[:, 0:384], ACT.Copy)
                    elif kind in ("cq0", "cq1"):
                        t, pair = jobs[n][1], int(kind[2])
                        e.activation(qo[:, t, 12 + 2 * pair:14 + 2 * pair, :].rearrange("p h x -> p (h x)"),
                                     ps[:, 0:256], ACT.Copy)
                        last = e.activation(qr_c[:, pair, t * P:(t + 1) * P], ps[:, 256:384], ACT.Copy)
                    elif kind == "kvc":
                        _, tt, pair = jobs[n]
                        e.activation(k_c[:, 2 * pair:2 * pair + 2, tt * P:(tt + 1) * P],
                                     ps[:, 0:256].rearrange("p (h x) -> p h x", h=2), ACT.Copy)
                        last = e.activation(kr_c[:, pair, tt * P:(tt + 1) * P], ps[:, 256:384], ACT.Copy)
                    else:
                        kt = key_tile[jobs[n][1]]
                        dst = (ckv_t if kind == "ckv" else k_ab[kind[0].upper()])[:, :, kt * P:(kt + 1) * P]
                        last = e.activation(dst, ps[:, 0:256].rearrange("p (h x) -> p h x", h=2), ACT.Copy)
                    last.then_inc(tp_read, 1)
                elif s[0] == "qk":
                    u = s[1]
                    g, h, t, keys, _ = attention_of(u)
                    nk = keys.stop - keys.start
                    scale = (192 if g == "C" else HD) ** -0.5
                    e.wait_ge(nmax_ready, u + 1)
                    if u >= 2:
                        e.wait_ge(tp_full, tp_no[("pt", u - 2)] + 1)
                    if g == "B":
                        e.activation(esink[u % 2], sink[:, h:h + 1], ACT.Exp, bias=nmx[u % 2])
                    e.activation(prob[u % 2][:, 0:nk], sc_ps[u % 2][:, 0:nk], ACT.Exp, bias=nmx[u % 2], scale=scale,
                                 accum_out=rsum[u % 2]).then_inc(e_ready, 1)
                elif s[0] == "pt":
                    u = s[1]
                    _, _, _, _, tiles = attention_of(u)
                    no = tp_no[s]
                    e.wait_ge(tp_full, no + 1)
                    if u >= 2:
                        e.wait_ge(o_full, u - 1)
                    e.activation(prob_t[u % 2][:, 0:len(tiles), :].rearrange("p a b -> p (a b)"),
                                 tp[no % 2][:, 0:len(tiles) * P], ACT.Copy).then_inc(tp_read, 1)
                elif s[0] == "out":
                    _, cc, t = s
                    n = cc * TILES + t
                    e.wait_ge(x1_ready, n + 1)
                    if n:
                        e.wait_ge(ss2_ready, n)
                    e.activation(junk2, x1[:, t, cc * 512:(cc + 1) * 512], ACT.Square,
                                 accum_out=ss2[:, 4 * t + cc:4 * t + cc + 1]).then_inc(ss2_ready, 1)
                    if cc == 3 and t:
                        h2_turned(t - 1)

            h2_turned(TILES - 1)
            e.wait_ge(ge_in, 1)
            e.activation(g_s, g_s, ACT.Exp).then_inc(ge_out, 1)
            e.wait_ge(re_in, 1)
            e.activation(tri3[:, 5, :], tri3[:, 4, :], ACT.Exp).then_inc(re_out, 1)

            def x_out(i):
                e.wait_ge(xt_full, i + 1)
                e.activation(xg_t[:, 0:4, :].rearrange("p a b -> p (a b)"), tp[0][:, :], ACT.Copy).then_inc(xt_read_a, 1)

            e.sem_inc(y_read_a, 1)
            x_out(0)
            e.wait_ge(tab_ready, 1)
            n = e.value_load(n_items[0:1, 0:1], min_val=EXPERTS, max_val=ITEMS - 1)
            with e.Fori(0, n) as i:
                e.wait_ge(h1_full, i + 1)
                e.wait_ge(act_ready, i + 1)
                e.activation(sg, acc[0][:, 0:256], ACT.Silu).then_inc(sg_ready, 1)
                e.wait_ge(h3_full, i + 1)
                x_out(i + 1)
                e.wait_ge(y_full, i + 2)
                e.activation(y_sb[:, 0, :], sc_ps[0][:, :], ACT.Copy, scale=w_tab[:, bass.ds(i, 1)])
                e.activation(y_part[:, 0, 0, :], sc_ps[0][:, :], ACT.Copy, scale=w_tab[:, bass.ds(i, 1)]).then_inc(y_read_a, 1)
                e.wait_ge(y_read_v, i + 2)
                e.activation(y_part[:, 0, 1, :], y_sb[:, 1, :], ACT.Copy).then_inc(y_upper, 1)
                for c in range(2):
                    e.wait_ge(y_rest, i * 2 + c + 1)
                    e.activation(y_part[:, 1, c, :], y_sb[:, c, :], ACT.Copy).then_inc(y_middle, 1)

        @block.vector
        def _(v):
            own = [0]

            def after(ins):
                own[0] += 1
                ins.then_inc(v_step, 1)
                v.wait_ge(v_step, own[0])

            v.memset(mod_ps[:, :], 0.0).then_inc(cleared, 1)
            for t in range(TILES):
                v.wait_ge(rx_ready, t + 1)
                v.tensor_scalar(xn[:, t, :], xn[:, t, :], rx[:, t:t + 1], None, ALU.mult).then_inc(xn_ready, 1)

            def bc(x, *shape):
                return x.to_broadcast([P, *shape])

            def rope(z, heads, pairs, cos, sin, out_sem=None):
                zp = z.rearrange("p h (c two) -> p h c two", two=2)
                e0, e1 = zp[:, :, :, 0], zp[:, :, :, 1]
                cb = cos.unsqueeze(1).to_broadcast([P, heads, pairs])
                sb_ = sin.unsqueeze(1).to_broadcast([P, heads, pairs])
                tmp = [rope_tmp[:, i, 0:heads * pairs].rearrange("p (h c) -> p h c", h=heads) for i in range(4)]
                v.tensor_tensor(tmp[0], e0, cb, ALU.mult)
                v.tensor_tensor(tmp[1], e1, sb_, ALU.mult)
                v.tensor_tensor(tmp[2], e0, sb_, ALU.mult)
                after(v.tensor_tensor(tmp[3], e1, cb, ALU.mult))
                v.tensor_tensor(e0, tmp[0], tmp[1], ALU.subtract)
                return v.tensor_tensor(e1, tmp[2], tmp[3], ALU.add)

            def tables(t, names):
                c, s_ = K(names[0]), K(names[1])
                w = c.shape[-1] // 2
                return c[:, (t - 1) * w:t * w], s_[:, (t - 1) * w:t * w]

            first_gain = [True]

            def key_rope(kt, tile):
                last = v.tensor_tensor(krg[:, kt, :], kr[:, kt, :], gain_of["c_kn"][:, HD:192], ALU.mult)
                if tile:
                    after(last)
                    last = rope(krg[:, kt:kt + 1, :], 1, 32, *tables(tile, ("cosr", "sinr")))
                v.tensor_scalar(kr_ss[:, kt:kt + 1], kr_ss[:, kt:kt + 1], 192 * EPS, None, ALU.add).then_inc(krg_ready, 1)

            def h2_turned(t):
                for b in (1, 3):
                    v.wait_ge(ht_full, 4 * t + b + 1)
                    v.tensor_copy(h2_t[t][:, 4 * b:4 * b + 4, :].rearrange("p a b -> p (a b)"),
                                  bank[4 + b][:, :]).then_inc(ht_read_v, 1)

            n_out = 0
            for s in steps:
                if s[0] == "mod" and s[2] == KD - 1:
                    g = s[1]
                    n = groups_order.index(g)
                    v.wait_ge(mod_done, n + 1)
                    v.wait_ge(row_in, rows_in(n))
                    v.tensor_tensor(mod_row[:], mod_ps[:, :], mod_row[:], ALU.add).then_inc(mod_read, 1)
                    if g in (SC1, SC2):
                        v.wait_ge(mod_read, n + 1)
                        v.scalar_tensor_tensor(out=mod_row[:], in0=mod_row[:], scalar=1.0, in1=gain_row[:],
                                               op0=ALU.add, op1=ALU.mult).then_inc(row_scaled, 1)
                elif s[0] == "modt":
                    n = s[1]
                    v.wait_ge(modt_full, n + 1)
                    v.tensor_copy(mod_t[:, n, :, :].rearrange("p b q -> p (b q)"),
                                  sc_ps[0][:, 32 * n:32 * n + 32]).then_inc(modt_ready, 1)
                elif s[0] == "hmod":
                    v.wait_ge(modt_ready, 2)
                    v.wait_ge(tp_read, KD)
                    for k in range(KD):
                        for c, cols in enumerate((slice(0, P), slice(P, T))):
                            at = 2 * (k // 4) + c
                            last = v.tensor_scalar(h_t[:, k, cols], h_t[:, k, cols], mod_t[:, 1, k % 4, at:at + 1],
                                                   mod_t[:, 0, k % 4, at:at + 1], ALU.mult, ALU.add)
                        last.then_inc(h_ready, 1)
                elif s[0] == "norm":
                    n = s[1]
                    kind, z, r = jobs[n][0], zt[n % 3], rstd[n % 3]
                    if n == 0:
                        v.wait_ge(gains_in, 10 * 16)
                    v.wait_ge(z_ready, n + 1)
                    v.wait_ge(rstd_ready, n + 1)

                    def scale_by(out, in_, i, gn):
                        return v.scalar_tensor_tensor(out=out, in0=in_, scalar=r[:, i:i + 1], in1=gn,
                                                      op0=ALU.mult, op1=ALU.mult)

                    if kind in ("aq0", "aq1", "bq0", "bq1", "akv", "bkv"):
                        heads = 3 if kind[1] == "q" else 2
                        gn = gain_of[kind[0] + ("_qn" if kind[1] == "q" else "_kn")]
                        for i in range(heads):
                            last = scale_by(z[:, i * HD:(i + 1) * HD], z[:, i * HD:(i + 1) * HD], i, gn)
                        if jobs[n][1]:
                            after(last)
                            last = rope(z[:, 0:heads * HD].rearrange("p (h x) -> p h x", h=heads), heads, 64,
                                        *tables(jobs[n][1], ("cos", "sin")))
                    elif kind in ("cq0", "cq1"):
                        for i in range(2):
                            scale_by(z[:, 384 + 64 * i:448 + 64 * i], z[:, i * 192 + HD:(i + 1) * 192], i,
                                     gain_of["c_qn"][:, HD:192])
                            last = scale_by(z[:, i * 192:i * 192 + HD], z[:, i * 192:i * 192 + HD], i,
                                            gain_of["c_qn"][:, 0:HD])
                        if jobs[n][1]:
                            after(last)
                            last = rope(z[:, 384:512].rearrange("p (h x) -> p h x", h=2), 2, 32,
                                        *tables(jobs[n][1], ("cosr", "sinr")))
                    elif kind == "ckv":
                        key_rope(key_tile[jobs[n][1]], jobs[n][1])
                        last = scale_by(z[:, 0:256], z[:, 0:256], 0, gain_of["c_kvn"])
                    else:
                        tt = jobs[n][1]
                        if n and jobs[n][2] == 0:
                            v.wait_ge(krg_ready, (1, 4, 2, 3)[tt])
                        for i in range(2):
                            scale_by(z[:, i * HD:(i + 1) * HD], z[:, i * HD:(i + 1) * HD], i, gain_of["c_kn"][:, 0:HD])
                            last = v.tensor_scalar(z[:, 256 + 64 * i:320 + 64 * i], krg[:, tt, :], r[:, i:i + 1], None, ALU.mult)
                    last.then_inc(norm_ready, 1)
                elif s == ("cache", "c"):
                    v.wait_ge(krss_ready, 1)
                    key_rope(1, 0)
                elif s[0] == "qk":
                    u = s[1]
                    g, h, t, keys, _ = attention_of(u)
                    nk = keys.stop - keys.start
                    b = u % 2
                    ps = sc_ps[b]
                    scale = (192 if g == "C" else HD) ** -0.5
                    v.wait_ge(s_full, u + 1)
                    if g == "B" and t:
                        lo = 2 * P if t == 1 else P
                        after(v.tensor_tensor(ps[:, lo:lo + P], ps[:, lo:lo + P], K("mask")[:, (t - 1) * P:t * P], ALU.add))
                    after(v.tensor_reduce(mx[b], ps[:, 0:nk], AX, ALU.max))
                    if g == "B":
                        after(v.tensor_scalar(mx[b], mx[b], scale, sink[:, h:h + 1], ALU.mult, ALU.max))
                        v.tensor_scalar(nmx[b], mx[b], -1.0, None, ALU.mult).then_inc(nmax_ready, 1)
                    else:
                        v.tensor_scalar(nmx[b], mx[b], -scale, None, ALU.mult).then_inc(nmax_ready, 1)
                elif s[0] == "nz":
                    u = s[1]
                    g, h, t, keys, _ = attention_of(u)
                    nk = keys.stop - keys.start
                    b = u % 2
                    v.wait_ge(e_ready, u + 1)
                    if g == "B":
                        after(v.tensor_tensor(rsum[b], rsum[b], esink[b], ALU.add))
                    after(v.reciprocal(rinv[b], rsum[b]))
                    v.tensor_scalar(prob[b][:, 0:nk], prob[b][:, 0:nk], rinv[b], None, ALU.mult).then_inc(p_ready, 1)
                elif s[0] == "pv":
                    u = s[1]
                    g, h, t, _, _ = attention_of(u)
                    hh = h + {"A": 0, "B": HEADS_A, "C": HEADS_A + HEADS_B}[g]
                    v.wait_ge(o_full, u + 1)
                    v.tensor_copy(qo[:, t, hh, :], tp[tp_no[("pt", u)] % 2][:, 384:512]).then_inc(o_ready, 1)
                elif s[0] == "out":
                    _, cc, t = s
                    cond = min(t, 1)
                    ps = acc[(n_jobs + n_out) % 3]
                    if n_out == 0:
                        v.wait_ge(g1_in, 2 * 16)
                        v.wait_ge(xres_in, 2 * 16)
                    v.wait_ge(acc_full, n_jobs + n_out + 1)
                    after(v.tensor_tensor(ps[:, :], ps[:, :], g1b[:, cond, cc * 512:(cc + 1) * 512], ALU.mult))
                    xs = x1[:, t, cc * 512:(cc + 1) * 512]
                    v.tensor_tensor(xs, ps[:, :], xs, ALU.add).then_inc(x1_ready, 1)
                    n_out += 1
                    if cc == 3:
                        if t:
                            h2_turned(t - 1)
                        v.wait_ge(ss2_ready, n_out)
                        v.tensor_reduce(ss2s[:, t:t + 1], ss2[:, 4 * t:4 * t + 4], AX, ALU.add).then_inc(ss2s_ready, 1)
                        v.wait_ge(r2_ready, t + 1)
                        if t == 0:
                            v.wait_ge(a2_in, 2 * 16)
                            v.wait_ge(sh2_in, 2 * 16)
                        after(v.scalar_tensor_tensor(out=h2[:, t, :], in0=x1[:, t, :], scalar=r2s[:, t:t + 1],
                                                     in1=a2b[:, cond, :], op0=ALU.mult, op1=ALU.mult))
                        v.tensor_tensor(h2[:, t, :], h2[:, t, :], sh2b[:, cond, :], ALU.add).then_inc(h2_ready, 1)

            h2_turned(TILES - 1)
            v.wait_ge(lg_full, 1)
            after(v.tensor_tensor(lg, lg_ps[:, 0:108].rearrange("p (t n) -> p t n", t=TILES),
                                  r_bias.unsqueeze(1).to_broadcast([P, TILES, 36]), ALU.add))
            gl, el = lg[:, :, 0:GROUPS], lg[:, :, GROUPS:]
            gmax, gsum, gp, m0, m1, d_, den, rden, vm = (tri3[:, i, :] for i in (0, 1, 2, 3, 6, 4, 7, 8, 9))
            r_ = tri3[:, 5, :]

            def b3(x, n):
                return x.unsqueeze(2).to_broadcast([P, TILES, n])

            after(v.tensor_reduce(gmax, gl, AX, ALU.max))
            v.tensor_tensor(g_s, gl, b3(gmax, GROUPS), ALU.subtract).then_inc(ge_in, 1)
            after(v.tensor_tensor(g_eq, gl, b3(gmax, GROUPS), ALU.is_equal))
            after(v.tensor_tensor(g_eq, g_eq, K("rev4").unsqueeze(1).to_broadcast([P, TILES, GROUPS]), ALU.mult))
            after(v.tensor_reduce(vm, g_eq, AX, ALU.max))
            after(v.tensor_tensor(g_oh, g_eq, b3(vm, GROUPS), ALU.is_equal))
            after(v.tensor_scalar(g_pen, g_oh, -1.0, -NEG, ALU.add, ALU.mult))
            grouped = el.rearrange("p t (g e) -> p t g e", g=GROUPS)
            after(v.tensor_tensor(sel.rearrange("p t (g e) -> p t g e", g=GROUPS), grouped,
                                  g_pen.unsqueeze(3).to_broadcast([P, TILES, GROUPS, PER_GROUP]), ALU.add))
            for k in range(TOP_K):
                m_ = (m0, m1)[k]
                o_ = oh[:, k * TILES:(k + 1) * TILES, :]
                after(v.tensor_reduce(m_, sel, AX, ALU.max))
                after(v.tensor_tensor(e_eq, sel, b3(m_, EXPERTS), ALU.is_equal))
                after(v.tensor_tensor(e_eq, e_eq, K("rev32").unsqueeze(1).to_broadcast([P, TILES, EXPERTS]), ALU.mult))
                after(v.tensor_reduce(vm, e_eq, AX, ALU.max))
                after(v.tensor_tensor(o_, e_eq, b3(vm, EXPERTS), ALU.is_equal))
                if k == 0:
                    after(v.scalar_tensor_tensor(out=sel, in0=o_, scalar=2 * NEG, in1=sel, op0=ALU.mult, op1=ALU.add))
            after(v.memset(oh_before[:, 0, :], 0.0))
            for c in range(ASSIGN):
                last = v.tensor_tensor(oh_before[:, c + 1, :], oh_before[:, c, :], oh[:, c, :], ALU.add)
                if c < ASSIGN - 1:
                    after(last)
            last.then_inc(oh_ready, 1)
            v.memset(xg, 0.0).then_inc(xg_clear, 1)
            weight = asg[:, 0, :]
            v.tensor_tensor(d_, m1, m0, ALU.subtract).then_inc(re_in, 1)
            v.wait_ge(ge_out, 1)
            after(v.tensor_reduce(gsum, g_s, AX, ALU.add))
            after(v.reciprocal(gp, gsum))
            v.wait_ge(re_out, 1)
            after(v.tensor_scalar(den, r_, 1.0, None, ALU.add))
            after(v.reciprocal(rden, den))
            after(v.tensor_tensor(weight[:, 0:TILES], gp, rden, ALU.mult))
            after(v.tensor_tensor(weight[:, TILES:ASSIGN], weight[:, 0:TILES], r_, ALU.mult))

            rank, exp_a, ovb, q_, slot_a, item_a, tmp6 = (asg[:, i, :] for i in range(1, 8))
            after(v.memset(zero32, 0.0))
            after(v.tensor_tensor(oh_tmp, oh, K("experts").unsqueeze(1).to_broadcast([P, ASSIGN, EXPERTS]), ALU.mult))
            after(v.tensor_reduce(exp_a, oh_tmp, AX, ALU.add))
            v.wait_ge(rank_full, 1)
            cnt = rank_ps[:, 192:224]
            after(v.tensor_tensor(oh_tmp, oh, rank_ps[:, 0:192].rearrange("p (a e) -> p a e", a=ASSIGN), ALU.mult))
            after(v.tensor_reduce(rank, oh_tmp, AX, ALU.add))
            def caps(n):
                return K("caps").unsqueeze(1).to_broadcast([P, n, MAX_Q - 1])

            after(v.tensor_tensor(beyond, cnt.unsqueeze(2).to_broadcast([P, EXPERTS, MAX_Q - 1]), caps(EXPERTS),
                                  ALU.is_gt))
            after(v.tensor_reduce(extra, beyond, AX, ALU.add))
            after(v.tensor_tensor_scan(extra_in, zero32, extra, 0.0, ALU.add, ALU.add))
            after(v.tensor_tensor(extra_ex, extra_in, extra, ALU.subtract))
            after(v.tensor_tensor(oh_tmp, oh, extra_ex.unsqueeze(1).to_broadcast([P, ASSIGN, EXPERTS]), ALU.mult))
            after(v.tensor_reduce(ovb, oh_tmp, AX, ALU.add))
            after(v.tensor_tensor(beyond[:, 0:ASSIGN, :], rank.unsqueeze(2).to_broadcast([P, ASSIGN, MAX_Q - 1]),
                                  caps(ASSIGN), ALU.is_ge))
            after(v.tensor_reduce(q_, beyond[:, 0:ASSIGN, :], AX, ALU.add))
            after(v.scalar_tensor_tensor(out=slot_a, in0=q_, scalar=-float(CAP), in1=rank, op0=ALU.mult, op1=ALU.add))
            after(v.tensor_tensor(tmp6, ovb, q_, ALU.add))
            after(v.scalar_tensor_tensor(out=tmp6, in0=tmp6, scalar=float(EXPERTS - 1), in1=exp_a,
                                         op0=ALU.add, op1=ALU.subtract))
            after(v.scalar_tensor_tensor(out=tmp6, in0=q_, scalar=1.0, in1=tmp6, op0=ALU.is_ge, op1=ALU.mult))
            after(v.tensor_tensor(item_a, exp_a, tmp6, ALU.add))

            def b6(x, n):
                return x.unsqueeze(2).to_broadcast([P, ASSIGN, n])

            v.tensor_tensor(at_slot, K("slots").unsqueeze(1).to_broadcast([P, ASSIGN, P]), b6(slot_a, P), ALU.is_equal)
            after(v.tensor_tensor(at_item, K("items").unsqueeze(1).to_broadcast([P, ASSIGN, ITEMS]),
                                  b6(item_a, ITEMS), ALU.is_equal))
            for i, x in enumerate((K("tok"), weight)):
                last = v.tensor_tensor(vals[:, :, i, :], at_item, b6(x, ITEMS), ALU.mult)
            last.then_inc(vals_ready, 1)
            n_over = ITEMS - EXPERTS
            v.tensor_copy(eid[0:1, 0:EXPERTS], K("experts")[0:1, :])
            after(v.tensor_scalar(eid[0:1, EXPERTS:], K("items")[0:1, 0:n_over], 0.0, None, ALU.add))
            after(v.tensor_tensor(over[0:1], extra_in[0:1].unsqueeze(1).to_broadcast([1, n_over, EXPERTS]),
                                  eid[0:1, EXPERTS:].unsqueeze(2).to_broadcast([1, n_over, EXPERTS]), ALU.is_le))
            after(v.tensor_reduce(eid[0:1, EXPERTS:], over[0:1], AX, ALU.add))
            after(v.tensor_scalar(eid[0:1, EXPERTS:], eid[0:1, EXPERTS:], float(EXPERTS - 1), None, ALU.min))
            v.tensor_copy(expert_of[:], eid[0:1, :])
            v.tensor_scalar(n_items[:], extra_in[0:1, EXPERTS - 1:EXPERTS], float(EXPERTS), None, ALU.add)
            v.wait_ge(tab_full, 1)
            v.tensor_scalar(row_f, tab_ps[:, 0:ITEMS], MISSING, 2.0, ALU.add, ALU.mult)
            v.tensor_scalar(tok_tab, tab_ps[:, 0:ITEMS], MISSING, None, ALU.add)
            after(v.tensor_copy(w_tab, tab_ps[:, ITEMS:2 * ITEMS]))
            v.tensor_scalar(row_tab, row_f, K("half"), None, ALU.add).then_inc(tab_ready, 1)

            def x_out(i):
                v.wait_ge(xt_full, i + 1)
                v.tensor_copy(xg_t[:, 4:8, :].rearrange("p a b -> p (a b)"), tp[1][:, :]).then_inc(xt_read_v, 1)

            def strip_of(k):
                c, ct = k // 2 % 2, k % 2
                return k // 4, slice(ct * HALF + c * 512, ct * HALF + (c + 1) * 512)

            def back(i, k):
                v.wait_ge(back_full, i * BACKS + k + 1)
                t, cols = strip_of(k)
                ct, strip = k % 2, y_sum[:, t, cols]
                v.tensor_tensor(strip, strip, (mod_ps, acc[2])[ct][:, :], ALU.add).then_inc(back_read, 1)

            after(v.memset(y_sb, 0.0))
            for n_part in range(3):
                v.tensor_copy(y_part[:, n_part, :, :], y_sb)
            v.tensor_copy(of_token, y_sb[:, 0, 0:T]).then_inc(y_split, 1)
            v.sem_inc(y_read_v, 1)
            v.sem_inc(act_ready, 1)
            v.sem_inc(at_read, 1)
            v.sem_inc(back_read, 2)
            x_out(0)
            v.wait_ge(tokens_in, 16)
            v.wait_ge(sum_clear, 1)
            v.wait_ge(tab_ready, 1)
            n = v.value_load(n_items[0:1, 0:1], min_val=EXPERTS, max_val=ITEMS - 1)
            with v.Fori(0, n) as i:
                v.wait_ge(back_read, i * BACKS + 2)
                for k in range(BACKS):
                    back(i, k)
                v.wait_ge(h3_full, i + 1)
                v.wait_ge(sg_ready, i + 1)
                v.wait_ge(at_full, i + 1)
                v.tensor_tensor(act, sg, acc[1][:, 0:256], ALU.mult).then_inc(act_ready, 1)
                x_out(i + 1)
                v.wait_ge(at_full, i + 2)
                v.wait_ge(y_full, i + 1)
                v.tensor_copy(act_t[:, :, :].rearrange("p a b -> p (a b)"), acc[2][:, 0:256]).then_inc(at_read, 1)
                v.tensor_scalar(of_token, tokens, tok_tab[:, bass.ds(i, 1)], None, ALU.is_equal)
                v.wait_ge(y_full, i + 2)
                v.tensor_scalar(y_sb[:, 1, :], sc_ps[1][:, :], w_tab[:, bass.ds(i, 1)], None, ALU.mult).then_inc(y_read_v, 1)
                v.wait_ge(y_read_a, i + 2)
                v.tensor_tensor(y_sb[:, 0, :], y_sb[:, 0, :], y_part[:, 0, 0, :], ALU.subtract).then_inc(y_rest, 1)
                v.wait_ge(y_upper, i + 1)
                v.tensor_tensor(y_sb[:, 1, :], y_sb[:, 1, :], y_part[:, 0, 1, :], ALU.subtract).then_inc(y_rest, 1)
                for c in range(2):
                    v.wait_ge(y_middle, i * 2 + c + 1)
                    last = v.tensor_tensor(y_part[:, 2, c, :], y_sb[:, c, :], y_part[:, 1, c, :], ALU.subtract)
                last.then_inc(y_split, 1)

            v.wait_ge(back_read, n * BACKS + 2)
            v.wait_ge(g2_in, 2 * 16)
            for k in range(BACKS + 1):
                if k < BACKS:
                    back(n, k)
                if k == 3:
                    v.wait_ge(back_read, n * BACKS + 6)
                    v.sem_inc(sum_ready, 1)
                if k > 4:
                    t, cols = strip_of(k - 1)
                    v.wait_ge(back_read, n * BACKS + k + 2)
                    after(v.tensor_tensor(y_sum[:, t, cols], y_sum[:, t, cols], g2b[:, 1, cols], ALU.mult))
                    last = v.tensor_tensor(x1[:, t, cols], x1[:, t, cols], y_sum[:, t, cols], ALU.add)
                    if k % 4 == 0:
                        last.then_inc(final_ready, 1)

        @block.gpsimd
        def _(g_):
            g = g_
            own = [0]

            def after(ins):
                own[0] += 1
                ins.then_inc(p_step, 1)
                g.wait_ge(p_step, own[0])

            def load_row(n):
                b = ins["b_mod"][0].rearrange("(g q n) -> g q n", g=6, q=4)[n]
                gn = ins["g_attn" if n < G1 else "g_ffn"][0].rearrange("(q n) -> q n", q=4)
                for c in range(2):
                    g.dma_start(mod_row[c:P:32, :], b).then_inc(row_in, 16)
                    if n in (SC1, SC2):
                        g.dma_start(gain_row[c:P:32, :], gn).then_inc(row_in, 16)

            def store_row(n):
                if n == SC2:
                    g.wait_ge(row_scaled, 2)
                else:
                    g.wait_ge(mod_read, n + 1)
                for c in range(2):
                    g.dma_start(mod_d[n, c].rearrange("(q n) -> q n", q=4), mod_row[c:P:32, :]).then_inc(row_out, 16)

            def power(dst, src, n):
                return g.tensor_tensor(dst, src, K("pow")[:, 0:n], ALU.pow)

            g.memset(gain_row[:], 0.0)
            after(g.memset(mod_row[:], 0.0))
            load_row(SH1)
            g.wait_ge(const_in, 16)
            for t in range(TILES):
                g.wait_ge(ssx_ready, t + 1)
                after(g.tensor_scalar(ssx[:, t:t + 1], ssx[:, t:t + 1], 1.0 / D, EPS, ALU.mult, ALU.add))
                power(rx[:, t:t + 1], ssx[:, t:t + 1], 1).then_inc(rx_ready, 1)
            for s in steps:
                if s[0] == "mod" and s[2] == KD - 1 and s[1] >= G1:
                    store_row(s[1])
                elif s[0] == "mod" and s[2] == 3 and s[1] > G1:
                    g.wait_ge(row_out, 32 * (s[1] - G1))
                    load_row(s[1])
                elif s[0] == "modt":
                    g.wait_ge(modt_full, s[1] + 1)
                    load_row(s[1] + 1)
                elif s[0] in ("proj", "kvc"):
                    n = s[1]
                    b, kind = n % 3, jobs[n][0]
                    heads, dim = {"ckv": (1, KV_RANK), "cq0": (2, 192), "cq1": (2, 192), "kvc": (2, 192),
                                  "akv": (2, HD), "bkv": (2, HD)}.get(kind, (3, HD))
                    sv = ss[b][:, 0:heads]
                    g.wait_ge(z_ready, n + 1)
                    if kind == "kvc":
                        tt = jobs[n][1]
                        g.wait_ge(krg_ready, (1, 4, 2, 3)[tt])
                        after(g.tensor_scalar(sv, sv, kr_ss[:, tt:tt + 1], 1.0 / dim, ALU.add, ALU.mult))
                    else:
                        after(g.tensor_scalar(sv, sv, 1.0 / dim, EPS, ALU.mult, ALU.add))
                    power(rstd[b][:, 0:heads], sv, heads).then_inc(rstd_ready, 1)
                elif s == ("cache", "a"):
                    g.wait_ge(o_full, 12)
                    for k in "ab":
                        g.dma_start(v_ab[k.upper()][:, 1, :, :], ins[f"cache_{k}_v"][0, 0]).then_inc(cache_v_in, 16)
                elif s[0] == "out":
                    _, cc, t = s
                    if (cc, t) == (0, 0):
                        g.wait_ge(acc_full, n_jobs)
                        g.dma_start(x1[:, 0, :], ins["x_prompt"][0]).then_inc(xres_in, 16)
                        g.dma_start(x1[:, 1:3, :], ins["x_sample"][0].rearrange("(t p) d -> p t d", p=P)).then_inc(xres_in, 16)
                        g.wait_ge(o_ready, n_atts)
                        g.wait_ge(state_out, 6 * 16)
                        for dst, n, done in ((g1b, G1, g1_in), (a2b, SC2, a2_in), (sh2b, SH2, sh2_in)):
                            for c in range(2):
                                g.dma_start(dst[:, c, :], mod_d[n, c].partition_broadcast(P)).then_inc(done, 16)
                        g.dma_start(w_r[:, :, 0:GROUPS], ins["w_rg"][0].rearrange("(p k) n -> p k n", k=KD)).then_inc(wr_in, 16)
                        g.dma_start(w_r[:, :, GROUPS:], ins["w_re"][0].rearrange("(p k) n -> p k n", k=KD)).then_inc(wr_in, 16)
                    if cc == 3:
                        g.wait_ge(ss2s_ready, t + 1)
                        after(g.tensor_scalar(ss2s[:, t:t + 1], ss2s[:, t:t + 1], 1.0 / D, EPS, ALU.mult, ALU.add))
                        power(r2s[:, t:t + 1], ss2s[:, t:t + 1], 1).then_inc(r2_ready, 1)
                        g.wait_ge(h2_ready, t + 1)
                        g.dma_start(h2_d[t * P:(t + 1) * P, :], h2[:, t, :]).then_inc(h2_out, 16)

            h2_rows = h2_d.rearrange("t (h n) -> (t h) n", h=2)
            gather_bound = g.to_reg(2 * T - 1)

            def gather():
                g.indirect_dma_start(out=xg, out_offset=None, in_=h2_rows,
                                     in_offset=bass.IndirectOffsetOnAxis(ap=gat_now[:], axis=0),
                                     bounds_check=gather_bound, oob_is_err=False).then_inc(xg_in, 16)

            g.wait_ge(row_out, 4 * 32)
            g.wait_ge(lg_full, 1)
            for c in range(2):
                g.dma_start(g2b[:, c, :], mod_d[G2, c].partition_broadcast(P)).then_inc(g2_in, 16)
            g.dma_start(tokens, ins["consts"][:, n_const:n_const + T]).then_inc(tokens_in, 16)
            g.wait_ge(h2_out, TILES * 16)
            g.wait_ge(tab_ready, 1)
            g.wait_ge(xg_clear, 1)
            after(g.tensor_copy(gat_now[:], row_tab[:, 0:1]))
            gather()
            g.memset(y_sum, 0.0).then_inc(sum_clear, 1)
            n = g.value_load(n_items[0:1, 0:1], min_val=EXPERTS, max_val=ITEMS - 1)
            with g.Fori(0, n) as i:
                g.wait_ge(xt_full, i + 1)
                g.wait_ge(xg_in, i * 16 + 16)
                g.tensor_copy(gat_now[:], row_tab[:, bass.ds(i + 1, 1)]).then_inc(gidx, 1)
                g.wait_ge(tab_ready, 1)
                g.wait_ge(gidx, i + 1)
                gather()
            g.wait_ge(x1_ready, 4 * TILES)
            g.wait_ge(sum_ready, 1)
            g.wait_ge(g2_in, 2 * 16)
            after(g.tensor_tensor(y_sum[:, 0, :], y_sum[:, 0, :], g2b[:, 0, :], ALU.mult))
            g.tensor_tensor(x1[:, 0, :], x1[:, 0, :], y_sum[:, 0, :], ALU.add).then_inc(final_ready_p, 1)


def kernel(**inputs):
    import concourse.bacc as bacc
    from concourse.bass_utils import run_bass_kernel_spmd as run

    nc = bacc.Bacc("TRN2", target_bir_lowering=False, num_devices=1)
    arrays = {f"in_{n}": np.ascontiguousarray(inputs[n]) for n in IN_NAMES}
    arrays["in_consts"] = constants()
    ins = {n[3:]: nc.dram_tensor(n, a.shape, mybir.dt.from_np(a.dtype), kind="ExternalInput").ap()
           for n, a in arrays.items()}
    outs = {n: nc.dram_tensor(f"out_{n}", s, F32, kind="ExternalOutput").ap() for n, s in OUTS}
    build(nc, ins, outs)
    r = run(nc, [arrays], core_ids=[0])
    return tuple(r.results[0][f"out_{n}"] for n, _ in OUTS)
```
